# Optimizing a Trainium2 kernel written in Bass

```python
import math
import jax, jax.numpy as jnp
from jax import lax
import numpy as np

D_MODEL = 1024
BATCH = 1
SEQ = 128
DEPTH = 1
DEC_BATCH = 1
DEC_SEQ = 512
PAST_LEN = 128

GRID_W = 64
N_HEADS = 4
D_QK = 64
D_V = 128
ATTN_W = N_HEADS * D_V
CONV_W = D_MODEL - ATTN_W
CONV_K = 3
IN_W = 3 * ATTN_W + 3 * CONV_W
N_GROUPS = 4
EXP_PER_GROUP = 4
N_EXPERTS = N_GROUPS * EXP_PER_GROUP
TOP_K = 2
D_EXPERT = 512
ROPE_BASE = 10000.0
Q_BLOCK = 128
EPS = 1e-6

kernel_name = "hymba_diffattn_shortconv_hiermoe_dit_step"

def rmsnorm(x, g):
    xf = x.astype(jnp.float32)
    y = xf * lax.rsqrt(jnp.mean(xf * xf, axis=-1, keepdims=True) + EPS)
    return (y * g.astype(jnp.float32)).astype(x.dtype)

def adaln(cond, w_mod, b_mod):
    m = jnp.einsum('nd,de->ne', jax.nn.silu(cond), w_mod) + b_mod
    return jnp.split(m[:, None, :], 6, axis=-1)

def axial_rope_tables(L):
    n_rows = L // GRID_W
    row = jnp.repeat(jnp.arange(n_rows), GRID_W).astype(jnp.float32)
    col = jnp.tile(jnp.arange(GRID_W), n_rows).astype(jnp.float32)
    nf = D_QK // 4
    inv = ROPE_BASE ** (-jnp.arange(nf, dtype=jnp.float32) / nf)
    ar = row[:, None] * inv
    ac = col[:, None] * inv
    ang = jnp.concatenate([ar, ar, ac, ac], axis=-1)
    return jnp.cos(ang), jnp.sin(ang)

def apply_axial_rope(x, cos, sin):
    x4 = x.reshape(x.shape[:-1] + (2, 2, D_QK // 4))
    rot = jnp.stack([-x4[..., 1, :], x4[..., 0, :]], axis=-2).reshape(x.shape)
    c = cos[:, None, :]
    s = sin[:, None, :]
    return (x.astype(jnp.float32) * c + rot.astype(jnp.float32) * s).astype(x.dtype)

def diff_attention(q, k, v, lam):
    B, H, Lq, _ = q.shape
    nb = Lq // Q_BLOCK
    scale = 1.0 / math.sqrt(D_QK)
    qb = q.reshape(B, H, nb, Q_BLOCK, 2 * D_QK).transpose(2, 0, 1, 3, 4)
    k1, k2 = k[..., :D_QK], k[..., D_QK:]

    def block(qi):
        s1 = jnp.einsum('bhqd,bhkd->bhqk', qi[..., :D_QK], k1).astype(jnp.float32) * scale
        s2 = jnp.einsum('bhqd,bhkd->bhqk', qi[..., D_QK:], k2).astype(jnp.float32) * scale
        p = jax.nn.softmax(s1, axis=-1) - lam * jax.nn.softmax(s2, axis=-1)
        return jnp.einsum('bhqk,bhkd->bhqd', p.astype(v.dtype), v)

    o = lax.map(block, qb)
    return o.transpose(1, 2, 0, 3, 4).reshape(B, H, Lq, D_V)

def short_conv(u, w):
    return lax.conv_general_dilated(
        u, w[:, None, :].astype(u.dtype), window_strides=(1,), padding=((1, 1),),
        dimension_numbers=('NWC', 'WIO', 'NWC'), feature_group_count=u.shape[-1])

def token_mixer(h, p, lam, lam_init, rope, ctx_kv):
    B, L, _ = h.shape
    z = jnp.einsum('bld,de->ble', h, p['w_in'])
    q, k, v, gb, gc, u = jnp.split(
        z, [ATTN_W, 2 * ATTN_W, 3 * ATTN_W, 3 * ATTN_W + CONV_W, 3 * ATTN_W + 2 * CONV_W], axis=-1)
    q = q.reshape(B, L, N_HEADS, 2, D_QK).transpose(0, 2, 1, 3, 4)
    k = k.reshape(B, L, N_HEADS, 2, D_QK).transpose(0, 2, 1, 3, 4)
    v = v.reshape(B, L, N_HEADS, D_V).transpose(0, 2, 1, 3)
    if rope is not None:
        q = apply_axial_rope(q, rope[0], rope[1])
        k = apply_axial_rope(k, rope[0], rope[1])
    q = q.reshape(B, N_HEADS, L, 2 * D_QK)
    k = k.reshape(B, N_HEADS, L, 2 * D_QK)
    if ctx_kv is not None:
        k_all = jnp.concatenate([ctx_kv[0].astype(k.dtype), k], axis=2)
        v_all = jnp.concatenate([ctx_kv[1].astype(v.dtype), v], axis=2)
    else:
        k_all, v_all = k, v
    o = diff_attention(q, k_all, v_all, lam)
    o = rmsnorm(o, p['subln_g']) * (1.0 - lam_init)
    o = o.transpose(0, 2, 1, 3).reshape(B, L, ATTN_W)
    y_conv = gb * short_conv(gc * u, p['conv_w'])
    out = jnp.einsum('ble,ed->bld', jnp.concatenate([o, y_conv], axis=-1), p['w_o'])
    return out, k, v

def hier_moe(h, p):
    B, L, D = h.shape
    t = h.reshape(B * L, D)
    pg = jax.nn.softmax(jnp.einsum('td,dg->tg', t, p['w_rg']).astype(jnp.float32), axis=-1)
    g_sel = jnp.argmax(pg, axis=-1)
    p_sel = jnp.max(pg, axis=-1, keepdims=True)
    le = jnp.einsum('td,de->te', t, p['w_re']).astype(jnp.float32).reshape(-1, N_GROUPS, EXP_PER_GROUP)
    le_sel = jnp.einsum('tg,tge->te', jax.nn.one_hot(g_sel, N_GROUPS, dtype=jnp.float32), le)
    wt, idx = lax.top_k(jax.nn.softmax(le_sel, axis=-1), TOP_K)
    wt = wt / jnp.sum(wt, axis=-1, keepdims=True) * p_sel
    eidx = g_sel[:, None] * EXP_PER_GROUP + idx
    gate = jnp.sum(jax.nn.one_hot(eidx, N_EXPERTS, dtype=jnp.float32) * wt[..., None], axis=1)
    y = jnp.zeros((B * L, D), jnp.float32)
    for e in range(N_EXPERTS):
        a = jax.nn.silu(t @ p['w_eg'][e]) * (t @ p['w_eu'][e])
        y = y + gate[:, e:e + 1] * (a @ p['w_ed'][e]).astype(jnp.float32)
    return y.astype(h.dtype).reshape(B, L, D)

def layer(x, mod, p, lam, lam_init, rope, ctx_kv):
    shift1, scale1, gate1, shift2, scale2, gate2 = mod
    h = rmsnorm(x, p['g_pre1']) * (1 + scale1) + shift1
    out, k, v = token_mixer(h, p, lam, lam_init, rope, ctx_kv)
    x = x + gate1 * rmsnorm(out, p['g_post1'])
    h = rmsnorm(x, p['g_pre2']) * (1 + scale2) + shift2
    x = x + gate2 * rmsnorm(hier_moe(h, p), p['g_post2'])
    return x, k, v

def setup_inputs(seed: int = 0) -> dict:
    key = jax.random.key(seed)
    ks = jax.random.split(key, 26)

    def nrm(k, shape, s):
        return jax.random.normal(k, shape, jnp.float32) * s

    D = D_MODEL
    return {
        "x_prompt": nrm(ks[0], (BATCH, SEQ, D), 1.0),
        "x_sample": nrm(ks[1], (DEC_BATCH, DEC_SEQ, D), 1.0),
        "cache_k": nrm(ks[2], (DEC_BATCH, DEPTH, N_HEADS, PAST_LEN, 2 * D_QK), 1.0),
        "cache_v": nrm(ks[3], (DEC_BATCH, DEPTH, N_HEADS, PAST_LEN, D_V), 1.0),
        "c": nrm(ks[4], (DEC_BATCH, D), 1.0),
        "c_ctx": nrm(ks[5], (D,), 1.0),
        "w_mod": nrm(ks[6], (DEPTH, D, 6 * D), 0.5 * D ** -0.5),
        "b_mod": nrm(ks[7], (DEPTH, 6 * D), 0.02),
        "g_pre1": 1.0 + nrm(ks[8], (DEPTH, D), 0.02),
        "g_post1": 1.0 + nrm(ks[9], (DEPTH, D), 0.02),
        "g_pre2": 1.0 + nrm(ks[10], (DEPTH, D), 0.02),
        "g_post2": 1.0 + nrm(ks[11], (DEPTH, D), 0.02),
        "w_in": nrm(ks[12], (DEPTH, D, IN_W), D ** -0.5),
        "conv_w": nrm(ks[13], (DEPTH, CONV_K, CONV_W), CONV_K ** -0.5),
        "lambda_q1": nrm(ks[14], (DEPTH, D_QK), 0.1),
        "lambda_k1": nrm(ks[15], (DEPTH, D_QK), 0.1),
        "lambda_q2": nrm(ks[16], (DEPTH, D_QK), 0.1),
        "lambda_k2": nrm(ks[17], (DEPTH, D_QK), 0.1),
        "subln_g": 1.0 + nrm(ks[18], (DEPTH, D_V), 0.02),
        "w_o": nrm(ks[19], (DEPTH, D, D), D ** -0.5),
        "w_router_group": nrm(ks[20], (DEPTH, D, N_GROUPS), D ** -0.5),
        "w_router_expert": nrm(ks[21], (DEPTH, D, N_EXPERTS), D ** -0.5),
        "w_exp_gate": nrm(ks[22], (DEPTH, N_EXPERTS, D, D_EXPERT), D ** -0.5),
        "w_exp_up": nrm(ks[23], (DEPTH, N_EXPERTS, D, D_EXPERT), D ** -0.5),
        "w_exp_down": nrm(ks[24], (DEPTH, N_EXPERTS, D_EXPERT, D), D_EXPERT ** -0.5),
    }

def reference(x_prompt, x_sample, cache_k, cache_v, c, c_ctx, w_mod, b_mod,
              g_pre1, g_post1, g_pre2, g_post2, w_in, conv_w,
              lambda_q1, lambda_k1, lambda_q2, lambda_k2, subln_g, w_o,
              w_router_group, w_router_expert, w_exp_gate, w_exp_up, w_exp_down):
    rope = axial_rope_tables(x_sample.shape[1])
    xp = x_prompt
    xs = x_sample
    new_k = []
    new_v = []
    for l in range(DEPTH):
        lam_init = 0.8 - 0.6 * math.exp(-0.3 * l)
        lam = (jnp.exp(jnp.sum(lambda_q1[l].astype(jnp.float32) * lambda_k1[l].astype(jnp.float32)))
               - jnp.exp(jnp.sum(lambda_q2[l].astype(jnp.float32) * lambda_k2[l].astype(jnp.float32)))
               + lam_init)
        p = {
            'w_in': w_in[l], 'w_o': w_o[l], 'conv_w': conv_w[l], 'subln_g': subln_g[l],
            'g_pre1': g_pre1[l], 'g_post1': g_post1[l], 'g_pre2': g_pre2[l], 'g_post2': g_post2[l],
            'w_rg': w_router_group[l], 'w_re': w_router_expert[l],
            'w_eg': w_exp_gate[l], 'w_eu': w_exp_up[l], 'w_ed': w_exp_down[l],
        }
        mod_ctx = adaln(c_ctx[None, :], w_mod[l], b_mod[l])
        mod_lat = adaln(c, w_mod[l], b_mod[l])
        xp, kp, vp = layer(xp, mod_ctx, p, lam, lam_init, None, None)
        new_k.append(kp)
        new_v.append(vp)
        xs, _, _ = layer(xs, mod_lat, p, lam, lam_init, rope, (cache_k[:, l], cache_v[:, l]))
    new_cache_k = jnp.stack(new_k, axis=1)
    new_cache_v = jnp.stack(new_v, axis=1)
    return (xp, xs, new_cache_k, new_cache_v)


_drawn_inputs = setup_inputs


def setup_inputs(seed=0):
    import zlib

    import numpy as np

    out = dict(_drawn_inputs(seed))
    spreads = {}
    factors = {'g_post2': 23.811, 'lambda_q1': 10.934}
    for name, (base, spread) in spreads.items():
        noise = np.random.default_rng([zlib.crc32(name.encode()), seed]).standard_normal(out[name].shape)
        drawn = base * np.exp(spread * noise) if base else spread * noise
        out[name] = __import__('jax').numpy.asarray(drawn.astype(out[name].dtype))
    for name, factor in factors.items():
        out[name] = (out[name] * factor).astype(out[name].dtype)
    return out
```

```python
import math
from contextlib import ExitStack

import concourse.bass as bass
from concourse import mybir

F32 = mybir.dt.float32
I32 = mybir.dt.int32
U32 = mybir.dt.uint32
ALU = mybir.AluOpType
ACT = mybir.ActivationFunctionType
AX = mybir.AxisListType.X

P = 128
D = 1024
KC = D // P
L_LAT, L_CTX, L_PAST = 512, 128, 128
TB = (L_LAT + L_CTX) // P
CTX = TB - 1
TOK = TB * P
H, DV, DQ = 4, 128, 64
KEYS = L_PAST + L_LAT
N = 512
NEXP, GROUPS, EPG, FE = 16, 4, 4, 512
EPS = 1e-6
SCALE = 1.0 / math.sqrt(DQ)
LAM_INIT = 0.8 - 0.6 * math.exp(-0.3 * 0)
BIG = 1e30

SLOTS_RING = 6
N_MOD, N_IN, N_O = 6 * D // N, 6, 2
MOD_EARLY = 4
N_PRE = N_MOD + N_IN + N_O
MAX_TILES = NEXP + (2 * TOK - 1) // P
MAX_PAIRS = (MAX_TILES + 1) // 2
XS_TILES = 2 * MAX_PAIRS + 1


def build(nc, a):
    w_mod = a["w_mod"].rearrange("l (k p) n -> p (l k) n", p=P)
    w_in = a["w_in"].rearrange("l (k p) n -> p (l k) n", p=P)
    w_o = a["w_o"].rearrange("l (k p) n -> p (l k) n", p=P)
    w_eg = a["w_exp_gate"].rearrange("l e (k p) n -> (l e) p k n", p=P)
    w_eu = a["w_exp_up"].rearrange("l e (k p) n -> (l e) p k n", p=P)
    w_ed = a["w_exp_down"].rearrange("l e (k p) n -> (l e) p k n", p=P)

    mod_d = nc.dram_tensor("mod_rows", [2, 6 * D], F32).ap()
    xs_d = nc.dram_tensor("expert_rows", [XS_TILES * P, D], F32).ap()
    os_d = xs_d

    ctx = ExitStack()
    with ctx:
        def sb(name, shape, dt=F32):
            return ctx.enter_context(nc.sbuf_tensor(name, shape, dt))

        def sem(name):
            return ctx.enter_context(nc.semaphore(name))

        ring = sb("weight_ring", [P, SLOTS_RING, KC * N])
        x = sb("x_rows", [P, TB, D])
        hT_mem = sb("hT_mem", [P, KC * TOK])
        catT_mem = sb("catT_mem", [P, KC * TOK])
        qkv = sb("qkv_mem", [P, 8 * D + 512])
        work = sb("work", [P, 2048])
        ident = sb("ident", [P, P])
        ones = sb("ones", [P, P])
        tri = sb("tri", [P, P])
        rope = sb("rope_tables", [P, 4, 2, DQ])
        small = sb("small", [P, 256])
        idx = sb("slot_index", [P, 2, TB], U32)
        steer = sb("steer", [1, 32], I32)
        iota = sb("iota_consts", [P, 64])
        wr = sb("router_weights", [P, KC, GROUPS + NEXP])
        ps = ctx.enter_context(nc.psum_tensor("ps", [P, 8, N], F32))
        psf = ps[:, :, :].rearrange("p b n -> p (b n)")

        hT = hT_mem[:, :].rearrange("p (k t) -> p k t", k=KC)
        h2 = hT_mem[:, :].rearrange("p (b d) -> p b d", b=TB)
        catT = catT_mem[:, :].rearrange("p (k t) -> p k t", k=KC)
        xn = qkv[:, 0:TB * D].rearrange("p (b d) -> p b d", b=TB)
        qT = qkv[:, 0:H * TOK].rearrange("p (h t) -> p h t", h=H)
        kT = qkv[:, 2560:2560 + H * 768].rearrange("p (h t) -> p h t", h=H)
        V = qkv[:, 5632:5632 + 6 * N].rearrange("p (b n) -> p b n", b=6)
        bc = qkv[:, 0:8 * D].rearrange("p (v c d) -> p v c d", v=4, c=2)

        def col(i, n=1):
            return small[:, i:i + n]
        condc = col(0, 16).rearrange("p (k c) -> p k c", c=2)
        condr = col(16, 16).rearrange("p (c k) -> p c k", c=2)
        gpre1 = col(32, 8)
        A1 = col(40, 16).rearrange("p (c k) -> p c k", c=2)
        B1 = col(56, 16).rearrange("p (c k) -> p c k", c=2)
        convw = col(72, 12).rearrange("p (t c) -> p t c", t=3)
        ssq, rt, rstd = col(84, 5), col(89, 5), col(94, 5)
        subg = col(99)
        nlam = col(100)
        epsc = col(101)
        lamw = col(102, 4)
        gate = col(106, 10).rearrange("p (j b) -> p j b", j=2)
        mx = col(116, 4).rearrange("p (u c) -> p u c", c=2)
        nm = col(120, 4).rearrange("p (u c) -> p u c", c=2)
        sm = col(124, 4).rearrange("p (u c) -> p u c", c=2)
        rc = col(128, 4).rearrange("p (u c) -> p u c", c=2)
        nr2 = col(132, 2)
        ss2, rt2, rs2 = col(134, 5), col(139, 5), col(144, 5)
        ss3, rt3, rs3 = col(149, 5), col(154, 5), col(159, 5)
        ss4, rt4, rs4 = col(164, 5), col(169, 5), col(174, 5)
        logit = sb("logits", [P, TB, GROUPS + NEXP])
        lamv = hT_mem[:, 0:4 * DQ].rearrange("p (v d) -> p v d", v=4)
        lamp = hT_mem[:, 4 * DQ:6 * DQ].rearrange("p (v d) -> p v d", v=2)

        loaded = [sem(f"panel_loaded{i}") for i in range(SLOTS_RING)]
        S = {n: sem(n) for n in (
            "x_lat_in x_ctx_in cond_in gpre_in convw_in subg_in lam_in rope_in ck_in cv_in wr_in "
            "consts silu_done sq1 rms1 xn_ready lam_prod lam_exp lam_ready "
            "mod_mm mod_row col_mm a1_ready modst0 modst1 modout0 modout1 h_tr hT_lat hT_ctx "
            "z_mm roped v_done qk_tr qkT conv_mm conv_c conv_u conv_y cache_out "
            "s_mm neg_max exp0 exp1 p_ready p_tr pt_act pt_dve pv_mm o_evac "
            "osq osq_mm osr onorm bc0 bc1 bc2 bc3 bc4 bc5 bc6 bc7 "
            "wo_mm sq2 rt2s x2s sq3 rt3s h2s h2_tr h2T_ev lg_mm "
            "oh_ready cum_mm slots steer_ready zero_src zeroed scattered "
            "xs_in0 xs_in1 xs_tr xT_act xT_dve g_mm u_mm sil act_a a_tr aT_ev dn_mm o_act o_dve os_out0 os_out1 "
            "gath0 gath1 ysq yrt yout y_dma dve_chain act_chain pool_chain").split()}

        pre = ([("mod", c) for c in range(MOD_EARLY)] + [("in", c) for c in range(N_IN)]
               + [("mod", c) for c in range(MOD_EARLY, N_MOD)] + [("o", c) for c in range(N_O)])
        place = {item: n for n, item in enumerate(pre)}

        def panel(n):
            return ring[:, n % SLOTS_RING, :].rearrange("p (k n) -> p k n", k=KC)

        def panel_ready(eng, n, i=0):
            eng.wait_ge(loaded[n % SLOTS_RING], 16 * (n // SLOTS_RING + 1) + i)

        def moe_panel(p, j):
            return N_PRE + 3 * p + j

        def mod_mem(c):
            m = catT_mem if c < MOD_EARLY else hT_mem
            b = 1536 * (c % 2) + (0 if c < MOD_EARLY else 1280 * 0)
            return (m[0:2, b:b + 512], m[0:2, b + 512:b + 1024], m[0:2, b + 1024:b + 1536])
        norm_of = {4: "g_post1", 5: "g_post1", 8: "g_pre2", 9: "g_pre2", 10: "g_post2", 11: "g_post2"}
        MODST = {}
        cnt = [0, 0]
        for c in range(N_MOD):
            cnt[c % 2] += 32 if c in norm_of else 16
            MODST[c] = cnt[c % 2]

        ck = catT_mem[:, 3072:3584].rearrange("p (h d) -> p h d", h=H)
        UNITS = [(h, b) for h in range(H) for b in range(TB)]

        def e_buf(u, c):
            return hT_mem[:, 1280 * (u % 2) + 640 * c:1280 * (u % 2) + 640 * c + 640]

        def p_buf(u):
            return hT_mem[:, 2560 + 640 * (u % 2):2560 + 640 * (u % 2) + 640]

        def pt_buf(u):
            return hT_mem[:, 3840 + 640 * (u % 2):3840 + 640 * (u % 2) + 640]

        xtile = [catT_mem[:, 0:1024], catT_mem[:, 1024:2048]]
        ostage = [catT_mem[:, 2048:3072], catT_mem[:, 3072:4096]]
        aT = catT_mem[:, 4096:4608].rearrange("p (k t) -> p k t", k=4)
        act_rows = catT_mem[:, 4608:5120]
        xT = work[:, 0:1024].rearrange("p (k t) -> p k t", k=KC)
        sil = work[:, 1024:1536]
        zero_rows = qkv[:, 8 * D:8 * D + 512]

        gathered = [sem(f"gathered{b}") for b in range(TB)]

        def qr(g):
            return work[:, 1024 + 512 * (g % 2):1536 + 512 * (g % 2)]
        Cst = work[:, 0:TOK]
        CU = work[:, 640:640 + TOK + 4]
        CUl, CUc = CU[:, 0:L_LAT + 2], CU[:, L_LAT + 2:TOK + 4]

        rw = {}
        at = [0]

        def rwork(name, n):
            rw[name] = work[:, 1024 + at[0]:1024 + at[0] + n]
            at[0] += n
        for name, n in (("gm", 5), ("eq", 20), ("oh", 20), ("dg", 20), ("eg", 20), ("sg", 5), ("ps", 5), ("E", 80),
                        ("o1", 80), ("o2", 80), ("m1", 5), ("m2", 5), ("d2", 5), ("e2", 5), ("t80", 80), ("f", 5),
                        ("A", 80), ("R", 80), ("nt", 16), ("st", 16), ("b2", 16), ("r", 5), ("bA", 5), ("bB", 5),
                        ("tt", 16), ("cmp", 160), ("tile", 16), ("np", 1), ("io8", 16), ("e128", 16)):
            rwork(name, n)
        assert at[0] <= 1024


        def yg(b, j):
            return ring[:, b, j * D:(j + 1) * D]

        block = ctx.enter_context(nc.Block())

        @block.sync
        def _(sp):
            def wait_used(n):
                kind, c = pre[n]
                if kind == "mod":
                    sp.wait_ge(S["mod_mm"], c + 1)
                elif kind == "o":
                    sp.wait_ge(S["wo_mm"], TB)
                elif c < 3:
                    sp.wait_ge(S["z_mm"], TB * (c + 1))
                else:
                    sp.wait_ge(S["conv_mm"], 12)

            sp.dma_start(x[:, 0:4, :], a["x_sample"].rearrange("b (t p) d -> p (b t) d", p=P)).then_inc(S["x_lat_in"], 16)
            sp.dma_start(x[:, CTX, :], a["x_prompt"][0, :, :]).then_inc(S["x_ctx_in"], 16)
            for n, (kind, c) in enumerate(pre):
                src = {"mod": w_mod, "in": w_in, "o": w_o}[kind]
                if n >= SLOTS_RING:
                    wait_used(n - SLOTS_RING)
                sp.dma_start(panel(n), src[:, :, c * N:(c + 1) * N]).then_inc(loaded[n % SLOTS_RING], 16)

            def expert_panels(p, e, i=None):
                for j, src in enumerate((w_eg, w_eu, w_ed)):
                    n = moe_panel(p, j)
                    s = n % SLOTS_RING
                    if i is None:
                        wait_used(n - SLOTS_RING)
                    else:
                        sp.wait_ge(S[("g_mm", "u_mm", "dn_mm")[j]], 2 * i + p + 1)
                    out = ring[:, s, :].rearrange("p (k n) -> p k n", k=KC if j < 2 else 4)
                    if i is None:
                        sp.dma_start(out, src[e, :, :, :]).then_inc(loaded[s], 16)
                    else:
                        sp.dma_start(out, src[bass.ds(e, 1), :, :, :].rearrange("a p k n -> p (a k) n")).then_inc(loaded[s], 16)

            expert_panels(0, 0)
            expert_panels(1, 1)
            sp.wait_ge(S["scattered"], 16 * 2 * TB)

            sp.dma_start(xtile[0], xs_d[0:P, :]).then_inc(S["xs_in0"], 16)
            sp.dma_start(xtile[1], xs_d[P:2 * P, :]).then_inc(S["xs_in1"], 16)
            sp.wait_ge(S["steer_ready"], 1)
            later = sp.value_load(steer[0:1, 30:31], min_val=NEXP // 2 - 1, max_val=MAX_PAIRS - 1)
            with sp.Fori(0, later) as i:
                for p in range(2):
                    sp.wait_ge(S["xs_tr"], 2 * i + p + 1)
                    sp.dma_start(xtile[p], xs_d[bass.ds(2 * P * i + (2 + p) * P, P), :]).then_inc(S[f"xs_in{p}"], 16)
                    e = sp.value_load(steer[0:1, bass.ds(2 * i + p + 2, 1)], min_val=0, max_val=NEXP - 1)
                    expert_panels(p, e, i)
            sp.wait_ge(S["xs_tr"], 2 * later + 1)
            sp.dma_start(xtile[0], xs_d[bass.ds(2 * P * later + 2 * P, P), :]).then_inc(S["xs_in0"], 16)

        @block.gpsimd
        def _(pool):
            pool.memset(ident[:, :], 0.0).then_inc(S["pool_chain"], 1)
            pool.memset(tri[:, :], 1.0).then_inc(S["pool_chain"], 1)
            pool.memset(ones[:, :], 1.0).then_inc(S["consts"], 1)
            pool.memset(epsc, EPS).then_inc(S["consts"], 1)
            pool.memset(col(181), 0.0).then_inc(S["os_out0"], 16)
            pool.memset(col(182), 0.0).then_inc(S["os_out1"], 16)
            pool.wait_ge(S["pool_chain"], 2)
            pool.affine_select(out=ident[:, :], in_=ident[:, :], compare_op=ALU.not_equal, fill=1.0, base=0,
                               pattern=[[-1, P]], channel_multiplier=1).then_inc(S["consts"], 1)
            pool.affine_select(out=tri[:, :], in_=tri[:, :], compare_op=ALU.is_gt, fill=0.0, base=0,
                               pattern=[[1, P]], channel_multiplier=-1).then_inc(S["consts"], 1)
            pool.iota(iota[:, 0:16], pattern=[[1, 16]], base=0, channel_multiplier=0,
                      allow_small_or_imprecise_dtypes=True).then_inc(S["consts"], 1)
            pool.wait_ge(S["wo_mm"], 1)
            pool.memset(zero_rows, 0.0).then_inc(S["zero_src"], 1)
            pool.wait_ge(S["zero_src"], 1)
            for t in range(XS_TILES):
                for j in range(2):
                    pool.dma_start(xs_d[t * P:(t + 1) * P, j * 512:(j + 1) * 512], zero_rows).then_inc(S["zeroed"], 16)
            pool.wait_ge(S["zeroed"], 32 * XS_TILES)
            pool.wait_ge(S["slots"], 1)
            for b in range(TB):
                for j in range(2):
                    pool.indirect_dma_start(out=xs_d[:, :], out_offset=bass.IndirectOffsetOnAxis(ap=idx[:, j, b:b + 1], axis=0),
                                            in_=h2[:, b, :], in_offset=None).then_inc(S["scattered"], 16)
            pool.wait_ge(S["steer_ready"], 1)
            pairs = pool.value_load(steer[0:1, 31:32], min_val=NEXP // 2, max_val=MAX_PAIRS)
            pool.wait_ge(S["os_out0"], 16 * pairs + 16)
            pool.wait_ge(S["os_out1"], 16 * pairs + 16)
            pool.tensor_tensor(col(180), epsc, epsc, ALU.add).then_inc(S["pool_chain"], 1)
            pool.wait_ge(S["pool_chain"], 3)
            for b in range(TB):
                for j in range(2):
                    pool.indirect_dma_start(out=yg(b, j), out_offset=None, in_=os_d[:, :],
                                            in_offset=bass.IndirectOffsetOnAxis(ap=idx[:, j, b:b + 1], axis=0)
                                            ).then_inc(gathered[b], 16)

        @block.scalar
        def _(act):
            n_chain = [0]

            def link(ins):
                n_chain[0] += 1
                ins.then_inc(S["act_chain"], 1)
                act.wait_ge(S["act_chain"], n_chain[0])

            with nc.allow_non_contiguous_dma(reason="vectors of the model dimension as columns"):
                act.dma_start(condr[:, 0, :], a["c"].rearrange("b (k p) -> p (b k)", p=P)).then_inc(S["cond_in"], 16)
                act.dma_start(condr[:, 1, :], a["c_ctx"].rearrange("(k p) -> p k", p=P)).then_inc(S["cond_in"], 16)

                def stage_mod(c):
                    brow, grow, _ = mod_mem(c)
                    act.dma_start(brow, a["b_mod"][:, c * N:(c + 1) * N].broadcast_to([2, N])).then_inc(S[f"modst{c % 2}"], 16)
                    if c in norm_of:
                        act.dma_start(grow, a[norm_of[c]][:, (c % 2) * N:(c % 2 + 1) * N].broadcast_to([2, N])).then_inc(S[f"modst{c % 2}"], 16)
                stage_mod(0)
                stage_mod(1)
                act.dma_start(gpre1, a["g_pre1"].rearrange("l (k p) -> p (l k)", p=P)).then_inc(S["gpre_in"], 16)
                for t in range(3):
                    act.dma_start(convw[:, t, :], a["conv_w"][0, t, :].rearrange("(c p) -> p c", p=P)).then_inc(S["convw_in"], 16)
                act.dma_start(subg, a["subln_g"].rearrange("l p -> p l")).then_inc(S["subg_in"], 16)
                for v, n in enumerate(("lambda_q1", "lambda_k1", "lambda_q2", "lambda_k2")):
                    act.dma_start(lamv[:, v, :], a[n].broadcast_to([P, DQ])).then_inc(S["lam_in"], 16)
                for t in range(2):
                    act.dma_start(rope[:, :, t, :], a["rope"][t, :, :].rearrange("(t p) d -> p t d", p=P)).then_inc(S["rope_in"], 16)
                act.dma_start(wr[:, :, 0:GROUPS], a["w_router_group"].rearrange("l (k p) n -> p (l k) n", p=P)).then_inc(S["wr_in"], 16)
                act.dma_start(wr[:, :, GROUPS:], a["w_router_expert"].rearrange("l (k p) n -> p (l k) n", p=P)).then_inc(S["wr_in"], 16)
                act.dma_start(ck, a["cache_k"].rearrange("b l h p d -> p (b l h) d")).then_inc(S["ck_in"], 16)
            act.wait_ge(S["cond_in"], 32)
            nc.scalar.activation(condc.rearrange("p k c -> p c k"), condr, ACT.Silu).then_inc(S["silu_done"], 1)
            act.wait_ge(S["x_lat_in"], 16)
            act.wait_ge(S["x_ctx_in"], 16)
            act.wait_ge(S["consts"], 5)
            for b in range(TB):
                ins = nc.scalar.activation(xn[:, b, :], x[:, b, :], ACT.Square, accum_out=ssq[:, b:b + 1])
            link(ins)
            nc.scalar.activation(rt, ssq, ACT.Sqrt, bias=epsc, scale=1.0 / D).then_inc(S["rms1"], 1)
            act.wait_ge(S["lam_prod"], 1)
            nc.scalar.activation(lamw[:, 2:4], lamw[:, 0:2], ACT.Exp).then_inc(S["lam_exp"], 1)
            for c in range(2, MOD_EARLY):
                act.wait_ge(S["mod_row"], c - 1)
                if c - 2 < MOD_EARLY:
                    act.wait_ge(S["col_mm"], c - 1)
                stage_mod(c)
            act.wait_ge(S["a1_ready"], 1)
            for k in range(KC):
                act.wait_ge(S["h_tr"], k + 1)
                nc.scalar.activation(hT[:, k, 0:L_LAT], ps[:, 2 * (k % 2), :], ACT.Identity,
                                     bias=B1[:, 0, k:k + 1], scale=A1[:, 0, k:k + 1]).then_inc(S["hT_lat"], 1)
            act.wait_ge(S["h_tr"], KC)
            act.dma_start(V[:, 0, :].rearrange("p (h d) -> p h d", h=H), a["cache_v"].rearrange("b l h p d -> p (b l h) d")).then_inc(S["cv_in"], 16)
            def qk_out(g):
                part, b = g // TB, g % TB
                act.wait_ge(S["qk_tr"], g + 1)
                dst = qT[:, :, b * P:(b + 1) * P] if part == 0 else kT[:, :, (b + 1) * P:(b + 2) * P]
                nc.scalar.copy(dst, ps[:, 2 + g % 2, :].rearrange("p (h t) -> p h t", h=H)).then_inc(S["qkT"], 1)
            for g in range(2 * TB):
                qk_out(g)
            for b in range(TB):
                act.wait_ge(S["z_mm"], 2 * TB + b + 1)
                nc.scalar.copy(V[:, b + 1, :], ps[:, (2 * TB + b) % 2, :]).then_inc(S["v_done"], 1)
            act.wait_ge(S["v_done"], TB)
            act.dma_start(a["out_v"].rearrange("b l h p d -> p (b l h) d"), V[:, TB, :].rearrange("p (h d) -> p h d", h=H)).then_inc(S["cache_out"], 16)
            act.wait_ge(S["roped"], 2 * TB)
            act.dma_start(a["out_k"].rearrange("b l h p d -> p (b l h) d"), qr(2 * TB - 1).rearrange("p (h d) -> p h d", h=H)).then_inc(S["cache_out"], 16)
            act.wait_ge(S["qk_tr"], 2 * TB + 1)
            nc.scalar.copy(kT[:, :, 0:P], ps[:, 6, :].rearrange("p (h t) -> p h t", h=H)).then_inc(S["qkT"], 1)
            for cb in range(4):
                act.wait_ge(S["conv_mm"], 3 * cb + 1)
                if cb >= 1:
                    act.wait_ge(S["conv_u"], 2 * cb)
                else:
                    act.wait_ge(S["qk_tr"], 2 * TB)
                    act.wait_ge(S["cache_out"], 32)
                nc.scalar.copy(Cst[:, 0:L_LAT], ps[:, 0, :]).then_inc(S["conv_c"], 1)
                nc.scalar.copy(Cst[:, L_LAT:TOK], ps[:, 1, 0:P]).then_inc(S["conv_c"], 1)
            def exps(u):
                h, b = UNITS[u]
                nk = KEYS if b < CTX else L_CTX
                for c in range(2):
                    act.wait_ge(S["neg_max"], 2 * u + c + 1)
                    if u >= 2 and c == 0:
                        act.wait_ge(S["p_ready"], u - 1)
                    nc.scalar.activation(e_buf(u, c)[:, 0:nk], psf[:, 1024 * c:1024 * c + nk], ACT.Exp,
                                         bias=nm[:, u % 2, c:c + 1], scale=SCALE,
                                         accum_out=sm[:, u % 2, c:c + 1]).then_inc(S[f"exp{c}"], 1)

            def pt_out(u):
                act.wait_ge(S["p_tr"], u + 1)
                if u >= 2:
                    act.wait_ge(S["pv_mm"], u - 1)
                nk = N if UNITS[u][1] < CTX else L_CTX
                nc.scalar.copy(pt_buf(u)[:, 0:nk], ps[:, 4, 0:nk]).then_inc(S["pt_act"], 1)

            def o_out(u):
                h, b = UNITS[u]
                act.wait_ge(S["pv_mm"], u + 1)
                nc.scalar.copy(catT[:, h, b * P:(b + 1) * P], ps[:, 6 + u % 2, 0:P]).then_inc(S["o_evac"], 1)
            for u in range(len(UNITS) + 2):
                if u < len(UNITS):
                    exps(u)
                if 1 <= u <= len(UNITS):
                    pt_out(u - 1)
                if u >= 2:
                    o_out(u - 2)
            stage_mod(4)
            stage_mod(5)
            for h in range(H):
                act.wait_ge(S["osq_mm"], h + 1)
                nc.scalar.activation(hT_mem[:, 3840:3840 + TOK], psf[:, 1024 * (h % 2):1024 * (h % 2) + TOK],
                                     ACT.Sqrt, bias=epsc, scale=1.0 / DV).then_inc(S["osr"], 1)
                if h < H - 1:
                    act.wait_ge(S["onorm"], h + 1)
            def send_mod(c):
                act.wait_ge(S["mod_row"], c + 1)
                act.dma_start(mod_d[:, c * N:(c + 1) * N], mod_mem(c)[2]).then_inc(S[f"modout{c % 2}"], 16)
            for c in range(MOD_EARLY, N_MOD):
                send_mod(c)
                if c + 2 < N_MOD:
                    stage_mod(c + 2)
            act.wait_ge(S["modout0"], 16 * (N_MOD - MOD_EARLY) // 2)
            act.wait_ge(S["modout1"], 16 * (N_MOD - MOD_EARLY) // 2)
            for v, off in enumerate((2 * D, 3 * D, 4 * D, 5 * D)):
                for c in range(2):
                    act.dma_start(bc[:, v, c, :], mod_d[c:c + 1, off:off + D].broadcast_to([P, D])).then_inc(S[f"bc{2 * v + c}"], 16)
            for b in range(TB):
                act.wait_ge(S["wo_mm"], b + 1)
                if b == 0:
                    act.wait_ge(S["modout0"], 16 * (N_MOD - MOD_EARLY) // 2)
                link(nc.scalar.activation(h2[:, b, :], psf[:, 1024 * (b % 2):1024 * (b % 2) + D], ACT.Square, accum_out=ss2[:, b:b + 1]))
                nc.scalar.activation(rt2[:, b:b + 1], ss2[:, b:b + 1], ACT.Sqrt, bias=epsc, scale=1.0 / D).then_inc(S["rt2s"], 1)
                act.wait_ge(S["x2s"], b + 1)
                link(nc.scalar.activation(h2[:, b, :], x[:, b, :], ACT.Square, accum_out=ss3[:, b:b + 1]))
                nc.scalar.activation(rt3[:, b:b + 1], ss3[:, b:b + 1], ACT.Sqrt, bias=epsc, scale=1.0 / D).then_inc(S["rt3s"], 1)
                act.wait_ge(S["h2_tr"], b + 1)
                if b >= 1:
                    act.wait_ge(S["lg_mm"], b)
                nc.scalar.copy(work[:, 0:1024], psf[:, 2048:3072]).then_inc(S["h2T_ev"], 1)
            act.wait_ge(S["oh_ready"], 1)
            nc.scalar.activation(rw["eg"], rw["dg"], ACT.Exp).then_inc(S["exp0"], 1)
            nc.scalar.activation(rw["e2"], rw["d2"], ACT.Exp).then_inc(S["exp0"], 1)
            act.wait_ge(S["steer_ready"], 1)
            act.wait_ge(S["scattered"], 16 * 2 * TB)
            act.wait_ge(S["xs_tr"], 1)
            nc.scalar.copy(xT.rearrange("p k t -> p (k t)")[:, 0:512], ps[:, 2, :]).then_inc(S["xT_act"], 1)
            pairs = act.value_load(steer[0:1, 31:32], min_val=NEXP // 2, max_val=MAX_PAIRS)
            with act.Fori(0, pairs) as i:
                for p in range(2):
                    act.wait_ge(S["g_mm"], 2 * i + p + 1)
                    nc.scalar.activation(sil, ps[:, 0, :], ACT.Silu).then_inc(S["sil"], 1)
                    act.wait_ge(S["xs_tr"], 2 * i + p + 2)
                    nc.scalar.copy(xT.rearrange("p k t -> p (k t)")[:, 0:512], ps[:, 2, :]).then_inc(S["xT_act"], 1)
                    act.wait_ge(S["a_tr"], 2 * i + p + 1)
                    nc.scalar.copy(aT.rearrange("p k t -> p (k t)"), ps[:, 4, :]).then_inc(S["aT_ev"], 1)
                    act.wait_ge(S["dn_mm"], 2 * i + p + 1)
                    act.wait_ge(S[f"os_out{p}"], 16 * i + 16)
                    nc.scalar.copy(ostage[p][:, 0:N], ps[:, 5, :]).then_inc(S["o_act"], 1)
                    act.wait_ge(S["o_act"], 2 * i + p + 1)
                    act.wait_ge(S["o_dve"], 2 * i + p + 1)
                    act.dma_start(os_d[bass.ds(2 * P * i + p * P, P), :], ostage[p]).then_inc(S[f"os_out{p}"], 16)
            for b in range(TB):
                act.wait_ge(S["ysq"], b + 1)
                link(nc.scalar.activation(yg(b, 1), yg(b, 0), ACT.Square, accum_out=ss4[:, b:b + 1]))
                nc.scalar.activation(rt4[:, b:b + 1], ss4[:, b:b + 1], ACT.Sqrt, bias=epsc, scale=1.0 / D).then_inc(S["yrt"], 1)
            for b in range(TB):
                act.wait_ge(S["yout"], b + 1)
                dst = a["out_lat"][0, b * P:(b + 1) * P, :] if b < CTX else a["out_ctx"][0, :, :]
                act.dma_start(dst, yg(b, 1)).then_inc(S["y_dma"], 16)
            act.wait_ge(S["y_dma"], 16 * TB)
            act.wait_ge(S["cache_out"], 32)

        @block.vector
        def _(dve):
            n_chain = [0]

            def link(ins):
                n_chain[0] += 1
                ins.then_inc(S["dve_chain"], 1)
                dve.wait_ge(S["dve_chain"], n_chain[0])

            tt, ts, stt = nc.vector.tensor_tensor, nc.vector.tensor_scalar, nc.vector.scalar_tensor_tensor
            dve.wait_ge(S["lam_in"], 64)
            link(tt(lamp, lamv[:, 0:4:2, :], lamv[:, 1:4:2, :], ALU.mult))
            nc.vector.reduce_sum(lamw[:, 0:2], lamp, axis=AX).then_inc(S["lam_prod"], 1)
            dve.wait_ge(S["rms1"], 1)
            link(nc.vector.reciprocal(rstd, rt))
            for b in range(TB):
                ts(xn[:, b, :], x[:, b, :], rstd[:, b:b + 1], None, ALU.mult).then_inc(S["xn_ready"], 1)
            dve.wait_ge(S["lam_exp"], 1)
            link(tt(nlam, lamw[:, 3:4], lamw[:, 2:3], ALU.subtract))
            link(ts(nlam, nlam, -LAM_INIT, None, ALU.add))

            def mod_row(c):
                brow, grow, row = mod_mem(c)
                dve.wait_ge(S["mod_mm"], c + 1)
                dve.wait_ge(S[f"modst{c % 2}"], MODST[c])
                if 2 <= c < MOD_EARLY:
                    dve.wait_ge(S["col_mm"], c - 1)
                if c >= MOD_EARLY + 2:
                    dve.wait_ge(S[f"modout{c % 2}"], 16 * ((c - MOD_EARLY) // 2))
                src = ps[0:2, 4 + c % 2, :]
                if c in norm_of:
                    link(tt(row, src, brow, ALU.add))
                    one = 1.0 if c in (8, 9) else 0.0
                    stt(row, row, one, grow, ALU.add, ALU.mult).then_inc(S["mod_row"], 1)
                else:
                    tt(row, src, brow, ALU.add).then_inc(S["mod_row"], 1)
            for c in range(MOD_EARLY):
                mod_row(c)
            dve.wait_ge(S["gpre_in"], 16)
            dve.wait_ge(S["col_mm"], MOD_EARLY)
            cols = ps[:, 6, 0:32].rearrange("p (s k c) -> p s c k", s=2, c=2)
            link(nc.vector.tensor_copy(B1, cols[:, 0, :, :]))
            link(stt(A1[:, 0, :], cols[:, 1, 0, :], 1.0, gpre1, ALU.add, ALU.mult))
            stt(A1[:, 1, :], cols[:, 1, 1, :], 1.0, gpre1, ALU.add, ALU.mult).then_inc(S["a1_ready"], 1)
            dve.wait_ge(S["a1_ready"], 1)
            for k in range(KC):
                dve.wait_ge(S["h_tr"], k + 1)
                ts(hT[:, k, L_LAT:TOK], ps[:, 2 * (k % 2) + 1, 0:P], A1[:, 1, k:k + 1], B1[:, 1, k:k + 1],
                   ALU.mult, ALU.add).then_inc(S["hT_ctx"], 1)
            dve.wait_ge(S["rope_in"], 32)
            for g in range(2 * TB):
                b = g % TB
                src = ps[:, g % 2, :]
                dve.wait_ge(S["z_mm"], g + 1)
                if g >= 2:
                    dve.wait_ge(S["qk_tr"], g - 1)
                if b == CTX:
                    nc.vector.tensor_copy(qr(g), src).then_inc(S["roped"], 1)
                    continue
                if g >= 1:
                    dve.wait_ge(S["roped"], g)
                t1 = work[:, 0:512]
                t2 = work[:, 512:1024]
                cos = rope[:, b, 0:1, :].broadcast_to([P, 8, DQ])
                sin = rope[:, b, 1, :].rearrange("p (a s d) -> p a s d", a=2, s=2)
                tt(t1.rearrange("p (g d) -> p g d", g=8), src.rearrange("p (g d) -> p g d", g=8), cos, ALU.mult).then_inc(S["dve_chain"], 1)
                n_chain[0] += 1
                sv = src.rearrange("p (g a s d) -> p g a s d", g=8, a=2, s=2)
                tv = t2.rearrange("p (g a s d) -> p g a s d", g=8, a=2, s=2)
                for s in range(2):
                    sn = sin[:, :, s, :].rearrange("p (o a) d -> p o a d", o=1).broadcast_to([P, 8, 2, 16])
                    ins = tt(tv[:, :, :, s, :], sv[:, :, :, 1 - s, :], sn, ALU.mult)
                    if s == 0:
                        ins.then_inc(S["dve_chain"], 1)
                        n_chain[0] += 1
                link(ins)
                tt(qr(g), t1, t2, ALU.add).then_inc(S["roped"], 1)
            dve.wait_ge(S["convw_in"], 48)
            dve.wait_ge(S["qk_tr"], 2 * TB)
            dve.wait_ge(S["cache_out"], 32)
            for edge in (CUl[:, 0:1], CUl[:, L_LAT + 1:L_LAT + 2], CUc[:, 0:1], CUc[:, L_CTX + 1:L_CTX + 2]):
                link(nc.vector.memset(edge, 0.0))
            for cb in range(4):
                dve.wait_ge(S["conv_c"], 2 * cb + 2)
                dve.wait_ge(S["conv_mm"], 3 * cb + 2)
                tt(CUl[:, 1:L_LAT + 1], ps[:, 2, :], Cst[:, 0:L_LAT], ALU.mult).then_inc(S["conv_u"], 1)
                tt(CUc[:, 1:L_CTX + 1], ps[:, 3, 0:P], Cst[:, L_LAT:TOK], ALU.mult).then_inc(S["conv_u"], 1)
                dve.wait_ge(S["conv_u"], 2 * cb + 2)
                for n, (buf, lo, ln) in enumerate(((CUl, 0, L_LAT), (CUc, L_LAT, L_CTX))):
                    y = catT[:, 4 + cb, lo:lo + ln]
                    link(ts(y, buf[:, 0:ln], convw[:, 0, cb:cb + 1], None, ALU.mult))
                    link(stt(y, buf[:, 1:ln + 1], convw[:, 1, cb:cb + 1], y, ALU.mult, ALU.add))
                    link(stt(y, buf[:, 2:ln + 2], convw[:, 2, cb:cb + 1], y, ALU.mult, ALU.add))
                    dve.wait_ge(S["conv_mm"], 3 * cb + 3)
                    tt(y, ps[:, 4 + n, 0:ln], y, ALU.mult).then_inc(S["conv_y"], 1)
            def maxes(u):
                nk = KEYS if UNITS[u][1] < CTX else L_CTX
                for c in range(2):
                    dve.wait_ge(S["s_mm"], 2 * u + c + 1)
                    link(nc.vector.reduce_max(mx[:, u % 2, c:c + 1], psf[:, 1024 * c:1024 * c + nk], axis=AX))
                    if u >= 2:
                        dve.wait_ge(S[f"exp{c}"], u - 1)
                    ts(nm[:, u % 2, c:c + 1], mx[:, u % 2, c:c + 1], -SCALE, None, ALU.mult).then_inc(S["neg_max"], 1)

            def combine(u):
                nk = KEYS if UNITS[u][1] < CTX else L_CTX
                dve.wait_ge(S["exp0"], u + 1)
                dve.wait_ge(S["exp1"], u + 1)
                link(nc.vector.reciprocal(rc[:, u % 2, :], sm[:, u % 2, :]))
                link(tt(nr2[:, u % 2:u % 2 + 1], rc[:, u % 2, 1:2], nlam, ALU.mult))
                e2 = e_buf(u, 1)[:, 0:nk]
                link(ts(e2, e2, nr2[:, u % 2:u % 2 + 1], None, ALU.mult))
                if u >= 2:
                    dve.wait_ge(S["p_tr"], u - 1)
                stt(p_buf(u)[:, 0:nk], e_buf(u, 0)[:, 0:nk], rc[:, u % 2, 0:1], e2, ALU.mult, ALU.add).then_inc(S["p_ready"], 1)

            def pt_out(u):
                if UNITS[u][1] == CTX:
                    return
                dve.wait_ge(S["p_tr"], u + 1)
                if u >= 2:
                    dve.wait_ge(S["pv_mm"], u - 1)
                nc.vector.tensor_copy(pt_buf(u)[:, N:KEYS], ps[:, 5, 0:P]).then_inc(S["pt_dve"], 1)
            for u in range(len(UNITS) + 1):
                if u < len(UNITS):
                    maxes(u)
                if u >= 1:
                    combine(u - 1)
                    pt_out(u - 1)
            dve.wait_ge(S["subg_in"], 16)
            dve.wait_ge(S["o_evac"], len(UNITS))
            sq = hT_mem[:, 3072:3072 + TOK]
            for h in range(H):
                if h >= 1:
                    dve.wait_ge(S["osq_mm"], h)
                tt(sq, catT[:, h, :], catT[:, h, :], ALU.mult).then_inc(S["osq"], 1)
                dve.wait_ge(S["osr"], h + 1)
                root = hT_mem[:, 3840:3840 + TOK]
                link(nc.vector.reciprocal(root, root))
                link(stt(catT[:, h, :], catT[:, h, :], subg, root, ALU.mult, ALU.mult))
                ts(catT[:, h, :], catT[:, h, :], 1.0 - LAM_INIT, None, ALU.mult).then_inc(S["onorm"], 1)
            for c in range(MOD_EARLY, N_MOD):
                mod_row(c)
            for b in range(TB):
                c = 1 if b == CTX else 0
                t = work[:, 1024:2048]
                if c == 1 or b == 0:
                    for v in range(4):
                        dve.wait_ge(S[f"bc{2 * v + c}"], 16)
                dve.wait_ge(S["rt2s"], b + 1)
                link(nc.vector.reciprocal(rs2[:, b:b + 1], rt2[:, b:b + 1]))
                link(stt(t, psf[:, 1024 * (b % 2):1024 * (b % 2) + D], rs2[:, b:b + 1], bc[:, 0, c, :], ALU.mult, ALU.mult))
                tt(x[:, b, :], x[:, b, :], t, ALU.add).then_inc(S["x2s"], 1)
                dve.wait_ge(S["rt3s"], b + 1)
                link(nc.vector.reciprocal(rs3[:, b:b + 1], rt3[:, b:b + 1]))
                link(stt(h2[:, b, :], x[:, b, :], rs3[:, b:b + 1], bc[:, 2, c, :], ALU.mult, ALU.mult))
                tt(h2[:, b, :], h2[:, b, :], bc[:, 1, c, :], ALU.add).then_inc(S["h2s"], 1)
            dve.wait_ge(S["lg_mm"], TB)
            dve.wait_ge(S["consts"], 5)
            link(nc.vector.tensor_copy(logit[:, :, :], ps[:, 6, 0:TB * 20].rearrange("p (b n) -> p b n", b=TB)))
            v3 = lambda name, b=TB: rw[name].rearrange("p (b n) -> p b n", b=b)
            bcast = lambda ap, n: ap.rearrange("p (b o) -> p b o", o=1).broadcast_to([P, TB, n])
            G, E16 = logit[:, :, 0:GROUPS], logit[:, :, GROUPS:]
            link(ts(rw["io8"], iota[:, 0:16], -1.0, 16.0, ALU.mult, ALU.add))
            link(ts(rw["e128"], iota[:, 0:16], float(P), None, ALU.mult))

            def first_max(out, vals, m, n):
                io = rw["io8"][:, 0:n].rearrange("p (o n) -> p o n", o=1).broadcast_to([P, TB, n])
                link(nc.vector.reduce_max(m, vals, axis=AX))
                link(tt(out, vals, bcast(m, n), ALU.is_equal))
                link(tt(out, out, io, ALU.mult))
                link(nc.vector.reduce_max(rw["f"], out, axis=AX))
                link(tt(out, out, bcast(rw["f"], n), ALU.is_equal))
            first_max(v3("oh"), G, rw["gm"], GROUPS)
            link(tt(v3("dg"), G, bcast(rw["gm"], GROUPS), ALU.subtract))
            oh4 = rw["oh"].rearrange("p (b g o) -> p b g o", b=TB, o=1).broadcast_to([P, TB, GROUPS, EPG])
            v4 = lambda ap: ap.rearrange("p b (g e) -> p b g e", g=GROUPS)
            link(tt(v4(v3("E")), v4(E16), oh4, ALU.mult))
            link(ts(v4(v3("t80")), oh4, -1.0, BIG, ALU.add, ALU.mult))
            link(tt(v3("E"), v3("E"), v3("t80"), ALU.add))
            first_max(v3("o1"), v3("E"), rw["m1"], NEXP)
            link(stt(v3("E"), v3("o1"), -4 * BIG, v3("E"), ALU.mult, ALU.add))
            first_max(v3("o2"), v3("E"), rw["m2"], NEXP)
            link(tt(v3("A"), v3("o1"), v3("o2"), ALU.add))
            tt(rw["d2"], rw["m2"], rw["m1"], ALU.subtract).then_inc(S["oh_ready"], 1)
            dve.wait_ge(S["exp0"], len(UNITS) + 2)
            link(nc.vector.reduce_sum(rw["sg"], v3("eg"), axis=AX))
            link(nc.vector.reciprocal(rw["ps"], rw["sg"]))
            link(ts(rw["m1"], rw["e2"], 1.0, None, ALU.add))
            link(nc.vector.reciprocal(rw["m2"], rw["m1"]))
            link(tt(gate[:, 0, :], rw["m2"], rw["ps"], ALU.mult))
            link(tt(gate[:, 1, :], gate[:, 0, :], rw["e2"], ALU.mult))
            dve.wait_ge(S["cum_mm"], 1)
            link(nc.vector.tensor_copy(v3("R"), ps[:, 7, 0:TB * 16].rearrange("p (b n) -> p b n", b=TB)))
            cntp = ps[:, 7, 80:96]
            link(ts(rw["nt"], cntp, float(P), None, ALU.is_gt))
            for j in range(2, 5):
                link(stt(rw["nt"], cntp, float(P * j), rw["nt"], ALU.is_gt, ALU.add))
            link(nc.vector.tensor_tensor_scan(rw["st"], ones[:, 0:16], rw["nt"], 0.0, ALU.mult, ALU.add))
            link(tt(rw["b2"], rw["st"], rw["nt"], ALU.subtract))
            link(ts(rw["b2"], rw["b2"], float(NEXP - 1), float(P), ALU.add, ALU.mult))
            for j, o in enumerate(("o1", "o2")):
                for out, w in (("r", v3("R")), ("bA", rw["e128"].rearrange("p (o n) -> p o n", o=1).broadcast_to([P, TB, 16])),
                               ("bB", rw["b2"].rearrange("p (o n) -> p o n", o=1).broadcast_to([P, TB, 16]))):
                    link(tt(v3("t80"), v3(o), w, ALU.mult))
                    link(nc.vector.reduce_sum(rw[out], v3("t80"), axis=AX))
                link(tt(rw["bB"], rw["bB"], rw["bA"], ALU.subtract))
                link(stt(rw["bB"], rw["r"], float(P), rw["bB"], ALU.is_ge, ALU.mult))
                link(tt(rw["bA"], rw["bA"], rw["bB"], ALU.add))
                link(tt(rw["r"], rw["r"], rw["bA"], ALU.add))
                link(nc.vector.tensor_copy(idx[:, j, :], rw["r"]))
            dve.wait_ge(S["h2s"], TB)
            nc.vector.tensor_copy(rw["np"], rw["gm"][:, 0:1]).then_inc(S["slots"], 1)
            cmp = rw["cmp"][0:1, :].rearrange("p (t e) -> p t e", t=10)
            link(tt(cmp, rw["st"][0:1, :].rearrange("p (o e) -> p o e", o=1).broadcast_to([1, 10, 16]),
                    iota[0:1, 0:10].rearrange("p (t o) -> p t o", o=1).broadcast_to([1, 10, 16]), ALU.is_le))
            link(nc.vector.reduce_sum(rw["tt"][0:1, 0:10], cmp, axis=AX))
            link(ts(rw["tt"][0:1, 0:10], rw["tt"][0:1, 0:10], float(NEXP - 1), None, ALU.min))
            link(nc.vector.memset(steer[:, :], 0))
            link(nc.vector.tensor_copy(steer[0:1, 16:26], rw["tt"][0:1, 0:10]))
            link(nc.vector.tensor_copy(steer[0:1, 0:16], iota[0:1, 0:16]))
            link(ts(rw["tile"][0:1, 0:5], iota[0:1, 0:5], 2.0, None, ALU.mult))
            link(tt(rw["tile"][0:1, 8:13], rw["st"][0:1, 15:16].broadcast_to([1, 5]), rw["tile"][0:1, 0:5], ALU.is_gt))
            link(nc.vector.reduce_sum(rw["np"][0:1, :], rw["tile"][0:1, 8:13], axis=AX))
            link(ts(rw["np"][0:1, :], rw["np"][0:1, :], float(NEXP // 2), None, ALU.add))
            link(nc.vector.tensor_copy(steer[0:1, 31:32], rw["np"][0:1, :]))
            link(ts(steer[0:1, 30:31], rw["np"][0:1, :], -1.0, None, ALU.add))
            nc.vector.tensor_copy(rw["np"], rw["gm"][:, 0:1]).then_inc(S["steer_ready"], 1)
            dve.wait_ge(S["steer_ready"], 1)
            dve.wait_ge(S["scattered"], 16 * 2 * TB)
            dve.wait_ge(S["xs_tr"], 1)
            nc.vector.tensor_copy(xT.rearrange("p k t -> p (k t)")[:, 512:1024], ps[:, 3, :]).then_inc(S["xT_dve"], 1)
            pairs = dve.value_load(steer[0:1, 31:32], min_val=NEXP // 2, max_val=MAX_PAIRS)
            with dve.Fori(0, pairs) as i:
                for p in range(2):
                    dve.wait_ge(S["sil"], 2 * i + p + 1)
                    dve.wait_ge(S["u_mm"], 2 * i + p + 1)
                    tt(act_rows, ps[:, 1, :], sil, ALU.mult).then_inc(S["act_a"], 1)
                    dve.wait_ge(S["xs_tr"], 2 * i + p + 2)
                    nc.vector.tensor_copy(xT.rearrange("p k t -> p (k t)")[:, 512:1024], ps[:, 3, :]).then_inc(S["xT_dve"], 1)
                    dve.wait_ge(S["dn_mm"], 2 * i + p + 1)
                    dve.wait_ge(S[f"os_out{p}"], 16 * i + 16)
                    nc.vector.tensor_copy(ostage[p][:, N:D], ps[:, 6, :]).then_inc(S["o_dve"], 1)
            for b in range(TB):
                dve.wait_ge(gathered[b], 32)
                link(ts(yg(b, 1), yg(b, 1), gate[:, 1, b:b + 1], None, ALU.mult))
                stt(yg(b, 0), yg(b, 0), gate[:, 0, b:b + 1], yg(b, 1), ALU.mult, ALU.add).then_inc(S["ysq"], 1)
            for b in range(TB):
                c = 1 if b == CTX else 0
                dve.wait_ge(S["yrt"], b + 1)
                link(nc.vector.reciprocal(rs4[:, b:b + 1], rt4[:, b:b + 1]))
                link(stt(yg(b, 0), yg(b, 0), rs4[:, b:b + 1], bc[:, 3, c, :], ALU.mult, ALU.mult))
                tt(yg(b, 1), yg(b, 0), x[:, b, :], ALU.add).then_inc(S["yout"], 1)

        @block.tensor
        def _(pe):
            mm = nc.tensor.matmul

            def mod(c):
                n = place["mod", c]
                panel_ready(pe, n)
                if c >= 2:
                    pe.wait_ge(S["mod_row"], c - 1)
                for k in range(KC):
                    ins = mm(ps[0:2, 4 + c % 2, :], condc[:, k, :], panel(n)[:, k, :], start=(k == 0), stop=(k == KC - 1))
                ins.then_inc(S["mod_mm"], 1)

            def mod_cols(c):
                pe.wait_ge(S["mod_row"], c + 1)
                for j in range(4):
                    o = (4 * c + j) * 2
                    ins = mm(ps[:, 6, o:o + 2], mod_mem(c)[2][:, j * P:(j + 1) * P], ident[0:2, 0:2], start=True, stop=True)
                ins.then_inc(S["col_mm"], 1)

            pe.wait_ge(S["consts"], 5)
            pe.wait_ge(S["silu_done"], 1)
            mod(0)
            for c in range(1, MOD_EARLY):
                mod(c)
                mod_cols(c - 1)
            mod_cols(MOD_EARLY - 1)
            pe.wait_ge(S["xn_ready"], TB)
            for k in range(KC):
                if k >= 2:
                    pe.wait_ge(S["hT_lat"], k - 1)
                    pe.wait_ge(S["hT_ctx"], k - 1)
                for b in range(4):
                    nc.tensor.transpose(ps[:, 2 * (k % 2), b * P:(b + 1) * P], xn[:, b, k * P:(k + 1) * P], ident[:, :])
                nc.tensor.transpose(ps[:, 2 * (k % 2) + 1, 0:P], xn[:, CTX, k * P:(k + 1) * P], ident[:, :]).then_inc(S["h_tr"], 1)
            pe.wait_ge(S["hT_lat"], KC)
            pe.wait_ge(S["hT_ctx"], KC)

            def transpose_rows(g):
                pe.wait_ge(S["roped"], g + 1)
                if g >= 2:
                    pe.wait_ge(S["qkT"], g - 1)
                for h in range(H):
                    ins = nc.tensor.transpose(ps[:, 2 + g % 2, h * P:(h + 1) * P], qr(g)[:, h * P:(h + 1) * P], ident[:, :])
                ins.then_inc(S["qk_tr"], 1)
            for g in range(3 * TB):
                part, b = g // TB, g % TB
                n = place["in", part]
                if b == 0:
                    panel_ready(pe, n)
                if 2 <= g < 2 * TB + 2:
                    pe.wait_ge(S["roped"], g - 1)
                elif g >= 2:
                    pe.wait_ge(S["v_done"], g - 2 * TB - 1)
                for k in range(KC):
                    ins = mm(ps[:, g % 2, :], hT[:, k, b * P:(b + 1) * P], panel(n)[:, k, :], start=(k == 0), stop=(k == KC - 1))
                ins.then_inc(S["z_mm"], 1)
                if 1 <= g <= 2 * TB:
                    transpose_rows(g - 1)
            pe.wait_ge(S["ck_in"], 16)
            for h in range(H):
                ins = nc.tensor.transpose(ps[:, 6, h * P:(h + 1) * P], ck[:, h, :], ident[:, :])
            ins.then_inc(S["qk_tr"], 1)
            pe.wait_ge(S["v_done"], TB)
            pe.wait_ge(S["qkT"], 2 * TB)
            for part in (3, 4, 5):
                panel_ready(pe, place["in", part])
            for cb in range(4):
                for j, part in enumerate((4, 5, 3)):
                    n = place["in", part]
                    if cb >= 1:
                        if j == 0:
                            pe.wait_ge(S["conv_c"], 2 * cb)
                        elif j == 1:
                            pe.wait_ge(S["conv_u"], 2 * cb)
                        else:
                            pe.wait_ge(S["conv_y"], 2 * cb)
                    for k in range(KC):
                        w = panel(n)[:, k, cb * P:(cb + 1) * P]
                        mm(ps[:, 2 * j, :], w, hT[:, k, 0:L_LAT], start=(k == 0), stop=(k == KC - 1))
                        ins = mm(ps[:, 2 * j + 1, 0:P], w, hT[:, k, L_LAT:TOK], start=(k == 0), stop=(k == KC - 1))
                    ins.then_inc(S["conv_mm"], 1)
            pe.wait_ge(S["qkT"], 2 * TB + 1)
            pe.wait_ge(S["cv_in"], 16)
            pe.wait_ge(S["conv_y"], 8)

            def scores(u):
                h, b = UNITS[u]
                for c in range(2):
                    if u >= 1:
                        pe.wait_ge(S[f"exp{c}"], u)
                    q = qT[c * DQ:(c + 1) * DQ, h, b * P:(b + 1) * P]
                    if b < CTX:
                        mm(ps[:, 2 * c, :], q, kT[c * DQ:(c + 1) * DQ, h, 0:N], start=True, stop=True)
                        ins = mm(ps[:, 2 * c + 1, 0:P], q, kT[c * DQ:(c + 1) * DQ, h, N:KEYS], start=True, stop=True)
                    else:
                        ins = mm(ps[:, 2 * c, 0:P], q, kT[c * DQ:(c + 1) * DQ, h, KEYS:KEYS + P], start=True, stop=True)
                    ins.then_inc(S["s_mm"], 1)

            def lat_units(u):
                return sum(1 for h, b in UNITS[:u + 1] if b < CTX)

            def p_transposes(u):
                nb = 5 if UNITS[u][1] < CTX else 1
                pe.wait_ge(S["p_ready"], u + 1)
                if u >= 1:
                    pe.wait_ge(S["pt_act"], u)
                    pe.wait_ge(S["pt_dve"], lat_units(u - 1))
                for j in range(nb):
                    ins = nc.tensor.transpose(ps[:, 4 + j // 4, (j % 4) * P:(j % 4 + 1) * P], p_buf(u)[:, j * P:(j + 1) * P], ident[:, :])
                ins.then_inc(S["p_tr"], 1)

            def pv(u):
                h, b = UNITS[u]
                pe.wait_ge(S["pt_act"], u + 1)
                pe.wait_ge(S["pt_dve"], lat_units(u))
                if u >= 2:
                    pe.wait_ge(S["o_evac"], u - 1)
                nb = 5 if b < CTX else 1
                for j in range(nb):
                    kb = j if b < CTX else 5
                    ins = mm(ps[:, 6 + u % 2, 0:P], V[:, kb, h * P:(h + 1) * P], pt_buf(u)[:, j * P:(j + 1) * P],
                             start=(j == 0), stop=(j == nb - 1))
                ins.then_inc(S["pv_mm"], 1)
            scores(0)
            for u in range(len(UNITS)):
                if u + 1 < len(UNITS):
                    scores(u + 1)
                p_transposes(u)
                if u >= 1:
                    pv(u - 1)
            pv(len(UNITS) - 1)
            pe.wait_ge(S["exp1"], len(UNITS))
            for h in range(H):
                pe.wait_ge(S["osq"], h + 1)
                if h >= 2:
                    pe.wait_ge(S["osr"], h - 1)
                sq = hT_mem[:, 3072:3072 + TOK]
                mm(ps[:, 2 * (h % 2), :], ones[:, :], sq[:, 0:N], start=True, stop=True)
                mm(ps[:, 2 * (h % 2) + 1, 0:P], ones[:, :], sq[:, N:TOK], start=True, stop=True).then_inc(S["osq_mm"], 1)
            pe.wait_ge(S["o_evac"], len(UNITS))
            for c in range(MOD_EARLY, N_MOD):
                mod(c)
            pe.wait_ge(S["onorm"], H)
            panel_ready(pe, place["o", 0])
            panel_ready(pe, place["o", 1])

            def router(b):
                pe.wait_ge(S["h2s"], b + 1)
                if b >= 1:
                    pe.wait_ge(S["h2T_ev"], b)
                for k in range(KC):
                    ins = nc.tensor.transpose(ps[:, 4 + k // 4, (k % 4) * P:(k % 4 + 1) * P], h2[:, b, k * P:(k + 1) * P], ident[:, :])
                ins.then_inc(S["h2_tr"], 1)
                pe.wait_ge(S["h2T_ev"], b + 1)
                for k in range(KC):
                    ins = mm(ps[:, 6, b * 20:(b + 1) * 20], work[:, k * P:(k + 1) * P], wr[:, k, :], start=(k == 0), stop=(k == KC - 1))
                ins.then_inc(S["lg_mm"], 1)
            pe.wait_ge(S["wr_in"], 32)
            pe.wait_ge(S["mod_row"], N_MOD)
            for b in range(TB):
                if b >= 2:
                    pe.wait_ge(S["x2s"], b - 1)
                for k in range(KC):
                    for j in range(2):
                        ins = mm(ps[:, 2 * (b % 2) + j, :], catT[:, k, b * P:(b + 1) * P], panel(place["o", j])[:, k, :],
                                 start=(k == 0), stop=(k == KC - 1))
                ins.then_inc(S["wo_mm"], 1)
                if b >= 1:
                    router(b - 1)
            router(TB - 1)
            pe.wait_ge(S["oh_ready"], 1)
            A = rw["A"].rearrange("p (b n) -> p b n", b=TB)
            for b in range(TB):
                for j in range(b):
                    mm(ps[:, 7, b * 16:(b + 1) * 16], ones[:, :], A[:, j, :], start=(j == 0), stop=False)
                mm(ps[:, 7, b * 16:(b + 1) * 16], tri[:, :], A[:, b, :], start=(b == 0), stop=True)
            for j in range(TB):
                ins = mm(ps[:, 7, 80:96], ones[:, :], A[:, j, :], start=(j == 0), stop=(j == TB - 1))
            ins.then_inc(S["cum_mm"], 1)
            def x_transposes(p):
                for k in range(KC):
                    ins = nc.tensor.transpose(ps[:, 2 + k // 4, (k % 4) * P:(k % 4 + 1) * P], xtile[p][:, k * P:(k + 1) * P], ident[:, :])
                ins.then_inc(S["xs_tr"], 1)
            pe.wait_ge(S["xs_in0"], 16)
            pe.wait_ge(S["steer_ready"], 1)
            x_transposes(0)
            pairs = pe.value_load(steer[0:1, 31:32], min_val=NEXP // 2, max_val=MAX_PAIRS)
            with pe.Fori(0, pairs) as i:
                for p in range(2):
                    t = 2 * i + p
                    slots = [moe_panel(p, j) for j in range(3)]
                    ready = lambda n: pe.wait_ge(loaded[n % SLOTS_RING], 16 * i + 16 * (n // SLOTS_RING + 1))
                    pe.wait_ge(S["xT_act"], t + 1)
                    pe.wait_ge(S["xT_dve"], t + 1)
                    for j in range(2):
                        ready(slots[j])
                        w = ring[:, slots[j] % SLOTS_RING, :].rearrange("p (k n) -> p k n", k=KC)
                        for k in range(KC):
                            ins = mm(ps[:, j, :], xT[:, k, :], w[:, k, :], start=(k == 0), stop=(k == KC - 1))
                        ins.then_inc(S[("g_mm", "u_mm")[j]], 1)
                    if p == 0:
                        pe.wait_ge(S["xs_in1"], 16 * i + 16)
                    else:
                        pe.wait_ge(S["xs_in0"], 16 * i + 32)
                    x_transposes(1 - p)
                    pe.wait_ge(S["act_a"], t + 1)
                    for k in range(4):
                        ins = nc.tensor.transpose(ps[:, 4, k * P:(k + 1) * P], act_rows[:, k * P:(k + 1) * P], ident[:, :])
                    ins.then_inc(S["a_tr"], 1)
                    pe.wait_ge(S["aT_ev"], t + 1)
                    ready(slots[2])
                    w = ring[:, slots[2] % SLOTS_RING, :].rearrange("p (k n) -> p k n", k=4)
                    for k in range(4):
                        for j in range(2):
                            ins = mm(ps[:, 5 + j, :], aT[:, k, :], w[:, k, j * N:(j + 1) * N], start=(k == 0), stop=(k == 3))
                    ins.then_inc(S["dn_mm"], 1)


_INS = ["x_prompt", "x_sample", "cache_k", "cache_v", "c", "c_ctx", "w_mod", "b_mod", "g_pre1", "g_post1", "g_pre2",
        "g_post2", "w_in", "conv_w", "lambda_q1", "lambda_k1", "lambda_q2", "lambda_k2", "subln_g", "w_o",
        "w_router_group", "w_router_expert", "w_exp_gate", "w_exp_up", "w_exp_down"]
_OUTS = [("out_ctx", (1, 128, 1024)), ("out_lat", (1, 512, 1024)),
         ("out_k", (1, 1, 4, 128, 128)), ("out_v", (1, 1, 4, 128, 128))]


def rope_tables():
    import numpy as np
    t = np.arange(L_LAT)
    inv = (np.float32(10000.0) ** (-np.arange(16, dtype=np.float32) / np.float32(16))).astype(np.float32)
    ar = (t // 64).astype(np.float32)[:, None] * inv
    ac = (t % 64).astype(np.float32)[:, None] * inv
    ang = np.concatenate([ar, ar, ac, ac], -1)
    sign = np.concatenate([-np.ones(16), np.ones(16)] * 2).astype(np.float32)
    return np.stack([np.cos(ang), np.sin(ang) * sign]).astype(np.float32)


def kernel(**inputs):
    import numpy as np
    import concourse.bacc as bacc
    from concourse.bass_utils import run_bass_kernel_spmd

    nc = bacc.Bacc("TRN2", target_bir_lowering=False, num_devices=1)
    arrays, aps = {}, {}
    for name in _INS:
        v = np.ascontiguousarray(inputs[name])
        arrays[f"in_{name}"] = v
        aps[name] = nc.dram_tensor(f"in_{name}", v.shape, mybir.dt.from_np(v.dtype), kind="ExternalInput").ap()
    arrays["rope"] = rope_tables()
    aps["rope"] = nc.dram_tensor("rope", arrays["rope"].shape, F32, kind="ExternalInput").ap()
    for name, shape in _OUTS:
        aps[name] = nc.dram_tensor(name, shape, F32, kind="ExternalOutput").ap()
    build(nc, aps)
    r = run_bass_kernel_spmd(nc, [arrays], core_ids=[0])
    return tuple(r.results[0][name] for name, _ in _OUTS)
```

```python
import math
from contextlib import ExitStack

import concourse.bass as bass
from concourse import mybir

F32 = mybir.dt.float32
F32R = mybir.dt.float32r
I32 = mybir.dt.int32
U32 = mybir.dt.uint32
ALU = mybir.AluOpType
ACT = mybir.ActivationFunctionType
AX = mybir.AxisListType.X

P = 128
D = 1024
KC = D // P
L_LAT, L_CTX, L_PAST = 512, 128, 128
TB = (L_LAT + L_CTX) // P
CTX = TB - 1
TOK = TB * P
H, DV, DQ = 4, 128, 64
KEYS = L_PAST + L_LAT
N = 512
NEXP, GROUPS, EPG, FE = 16, 4, 4, 512
EPS = 1e-6
SCALE = 1.0 / math.sqrt(DQ)
LAM_INIT = 0.8 - 0.6 * math.exp(-0.3 * 0)
BIG = 1e30

N_MOD, N_IN, N_O = 6 * D // N, 3, 2
MOD_EARLY = 4
RAW, SPLIT = 4, 8
QUARTER = 2 * N
MAX_TILES = NEXP + (2 * TOK - 1) // P
MAX_PAIRS = (MAX_TILES + 1) // 2
XS_TILES = 2 * MAX_PAIRS + 1
MOE_RAW = 8


def build(nc, a):
    w_mod = a["w_mod"].rearrange("l (k p) n -> p (l k) n", p=P)
    w_in = a["w_in"].rearrange("l (k p) n -> p (l k) n", p=P)
    w_o = a["w_o"].rearrange("l (k p) n -> p (l k) n", p=P)
    w_eg = a["w_exp_gate"].rearrange("l e (k p) n -> (l e) p k n", p=P)
    w_eu = a["w_exp_up"].rearrange("l e (k p) n -> (l e) p k n", p=P)
    w_ed = a["w_exp_down"].rearrange("l e (k p) n -> (l e) p k n", p=P)

    mod_d = nc.dram_tensor("mod_rows", [2, 6 * D], F32).ap()
    xs_d = nc.dram_tensor("expert_rows", [XS_TILES * P, D], F32).ap()
    os_d = xs_d

    ctx = ExitStack()
    with ctx:
        def sb(name, shape, dt=F32):
            return ctx.enter_context(nc.sbuf_tensor(name, shape, dt))

        def sem(name):
            return ctx.enter_context(nc.semaphore(name))

        raw = sb("raw_ring", [P, RAW, QUARTER])
        spl = sb("split_ring", [P, SPLIT, 2, QUARTER], F32R)
        hs = sb("split_rows", [P, 2, KC * TOK], F32R)
        conds = sb("split_cond", [P, 2, KC, 2], F32R)
        x = sb("x_rows", [P, TB, D])
        catT_mem = sb("catT_mem", [P, KC * TOK])
        qkv = sb("qkv_mem", [P, 8 * D + 512])
        work = sb("work", [P, 2048])
        ident = sb("ident", [P, P])
        ones = sb("ones", [P, P])
        tri = sb("tri", [P, P])
        small = sb("small", [P, 256])
        idx = sb("slot_index", [P, 2, TB], U32)
        steer = sb("steer", [1, 32], I32)
        iota = sb("iota_consts", [P, 64])
        wr = sb("router_weights", [P, KC, GROUPS + NEXP])
        ps = ctx.enter_context(nc.psum_tensor("ps", [P, 8, N], F32))
        psf = ps[:, :, :].rearrange("p b n -> p (b n)")

        hT_mem = x[:, :, :].rearrange("p b d -> p (b d)")
        h2 = catT_mem[:, :].rearrange("p (b d) -> p b d", b=TB)
        hS = hs[:, :, :].rearrange("p c (k t) -> p c k t", k=KC)
        rope = catT_mem[:, 3584:4096].rearrange("p (b c d) -> p b c d", b=4, c=2)
        catT = catT_mem[:, :].rearrange("p (k t) -> p k t", k=KC)
        xn = qkv[:, 0:TB * D].rearrange("p (b d) -> p b d", b=TB)
        qT = qkv[:, 0:H * TOK].rearrange("p (h t) -> p h t", h=H)
        kT = qkv[:, 2560:2560 + H * 768].rearrange("p (h t) -> p h t", h=H)
        V = qkv[:, 5632:5632 + 6 * N].rearrange("p (b n) -> p b n", b=6)
        bc = qkv[:, 0:8 * D].rearrange("p (v c d) -> p v c d", v=4, c=2)

        def col(i, n=1):
            return small[:, i:i + n]
        condc = col(0, 16).rearrange("p (k c) -> p k c", c=2)
        condr = col(16, 16).rearrange("p (c k) -> p c k", c=2)
        gpre1 = col(32, 8)
        A1 = col(40, 16).rearrange("p (c k) -> p c k", c=2)
        B1 = col(56, 16).rearrange("p (c k) -> p c k", c=2)
        convw = col(72, 12).rearrange("p (t c) -> p t c", t=3)
        ssq, rt, rstd = col(84, 5), col(89, 5), col(94, 5)
        subg = col(99)
        nlam = col(100)
        epsc = col(101)
        lamw = col(102, 4)
        gate = col(106, 10).rearrange("p (j b) -> p j b", j=2)
        mx = col(116, 4).rearrange("p (u c) -> p u c", c=2)
        nm = col(120, 4).rearrange("p (u c) -> p u c", c=2)
        sm = col(124, 4).rearrange("p (u c) -> p u c", c=2)
        rc = col(128, 4).rearrange("p (u c) -> p u c", c=2)
        nr2 = col(132, 2)
        ss2, rt2, rs2 = col(134, 5), col(139, 5), col(144, 5)
        ss3, rt3, rs3 = col(149, 5), col(154, 5), col(159, 5)
        ss4, rt4, rs4 = col(164, 5), col(169, 5), col(174, 5)
        logit = sb("logits", [P, TB, GROUPS + NEXP])
        lamv = work[:, 1280:1280 + 4 * DQ].rearrange("p (v d) -> p v d", v=4)
        lamp = work[:, 1536:1536 + 2 * DQ].rearrange("p (v d) -> p v d", v=2)

        rawl = [sem(f"raw_loaded{i}") for i in range(MOE_RAW)]
        S = {n: sem(n) for n in (
            "x_lat_in x_ctx_in cond_in gpre_in convw_in subg_in lam_in rope_in ck_in cv_in wr_in "
            "hi lo x_again conds_hi conds_lo hf_lat hf_ctx cat_hi cat_lo xT_lo aT_lo consts silu_done sq1 rms1 xn_ready lam_prod lam_exp lam_ready "
            "mod_mm mod_row col_mm a1_ready modst0 modst1 modout0 modout1 h_tr hT_lat hT_ctx "
            "z_mm roped v_done qk_tr qkT conv_mm conv_c conv_u conv_y cache_out "
            "s_mm neg_max exp0 exp1 p_ready p_tr pt_act pt_dve pv_mm o_evac "
            "osq osq_mm osr onorm bc0 bc1 bc2 bc3 bc4 bc5 bc6 bc7 "
            "wo_mm sq2 rt2s x2s sq3 rt3s h2s h2_tr h2T_ev lg_mm "
            "oh_ready cum_mm slots steer_ready zero_src zeroed scattered "
            "xs_in0 xs_in1 xs_tr xT_act xT_dve g_mm u_mm sil act_a a_tr aT_ev dn_mm o_act o_dve os_out0 os_out1 "
            "gath0 gath1 ysq yrt yout y_dma dve_chain act_chain pool_chain").split()}

        pre = ([("mod", c) for c in range(MOD_EARLY)] + [("in", c) for c in range(N_IN)]
               + [("conv", c) for c in range(4)]
               + [("mod", c) for c in range(MOD_EARLY, N_MOD)] + [("o", c) for c in range(N_O)])
        place = {item: n for n, item in enumerate(pre)}
        PRE_Q = 4 * len(pre)
        assert PRE_Q % RAW == 0
        raw_count, raw_value = [0] * RAW, []
        for q in range(PRE_Q):
            raw_count[q % RAW] += 48 if pre[q // 4][0] == "conv" else 16
            raw_value.append(raw_count[q % RAW])

        def weight(n, k, c, lo=0, hi=N):
            o = (k % 2) * N
            return spl[:, (4 * n + k // 2) % SPLIT, c, o + lo:o + hi]

        def conv_weight(n, k, c, part):
            o = (k % 2) * 3 * P + part * P
            return spl[:, (4 * n + k // 2) % SPLIT, c, o:o + P]

        def used(eng, n):
            kind, c = pre[n]
            if kind == "mod":
                eng.wait_ge(S["mod_mm"], c + 1)
            elif kind == "o":
                eng.wait_ge(S["wo_mm"], TB)
            elif kind == "in":
                eng.wait_ge(S["z_mm"], TB * (c + 1))
            else:
                eng.wait_ge(S["conv_mm"], 3 * (c + 1))

        def lin(tile, a, b):
            i, c = tile
            return a * c + b if i is None else i * (2 * a) + (a * c + b)

        def pos(tile, j, r):
            return 12 * tile[1] - 4 + 4 * j + r + (4 if tile[0] is None and tile[1] == 0 else 0)

        def moe_split_slot(tile, j, r):
            return (PRE_Q + pos(tile, j, r)) % SPLIT

        def moe_raw(tile, j, r):
            n = pos(tile, j, r) % MOE_RAW
            return raw[:, n, :] if n < RAW else bc[:, 1 + (n - RAW) // 2, (n - RAW) % 2, :]

        def moe_lo(tile, j, r):
            n = PRE_Q + pos(tile, j, r) + 1
            return n if tile[0] is None else tile[0] * 24 + n

        def moe_loaded(tile, j, r):
            n = pos(tile, j, r)
            v = (raw_count[n % MOE_RAW] if n % MOE_RAW < RAW else 0) + 16 * (n // MOE_RAW + 1)
            return v if tile[0] is None else tile[0] * 48 + v

        def mod_mem(c):
            if c < MOD_EARLY:
                m, b = catT_mem, 1536 * (c % 2)
            else:
                m, b = (hT_mem, 2560) if c % 2 == 0 else (work, 0)
            return (m[0:2, b:b + 512], m[0:2, b + 512:b + 1024], m[0:2, b + 1024:b + 1536])
        norm_of = {4: "g_post1", 5: "g_post1", 8: "g_pre2", 9: "g_pre2", 10: "g_post2", 11: "g_post2"}
        MODST = {}
        cnt = [0, 0]
        for c in range(N_MOD):
            cnt[c % 2] += 32 if c in norm_of else 16
            MODST[c] = cnt[c % 2]

        ck = catT_mem[:, 3072:3584].rearrange("p (h d) -> p h d", h=H)
        def cat_ready(k):
            return (S["conv_y"], 2 * (k - H + 1)) if k >= H else (S["onorm"], k + 1)
        UNITS = [(h, b) for h in range(H) for b in range(TB)]
        ROOT_STEP = {TB * (h + 1) + 1: h for h in range(H - 1)}
        CAT_ORDER = [4, 5, 6, 7, 0, 1, 2, 3]

        def e_buf(u, c):
            return hT_mem[:, 640 * c:640 * c + 640]

        def p_buf(u):
            return hT_mem[:, 1280:1920]

        def pt_buf(u):
            return hT_mem[:, 1920:2560]
        osq_buf = hT_mem[:, 4096:4096 + TOK]

        xtile = [catT_mem[:, 0:1024], catT_mem[:, 1024:2048]]
        ostage = [catT_mem[:, 2048:3072], catT_mem[:, 3072:4096]]
        act_rows = catT_mem[:, 4608:5120]
        xS = hs[:, :, 0:1024].rearrange("p c (k t) -> p c k t", k=KC)
        aS = hs[:, :, 1024:1536].rearrange("p c (k t) -> p c k t", k=4)
        sil = work[:, 1024:1536]
        zero_rows = work[:, 1536:2048]

        gathered = [sem(f"gathered{b}") for b in range(TB)]

        def qr(g):
            return work[:, 1024 + 512 * (g % 2):1536 + 512 * (g % 2)]
        Cst = work[:, 0:TOK]
        CU = work[:, 640:640 + TOK + 4]
        CUl, CUc = CU[:, 0:L_LAT + 2], CU[:, L_LAT + 2:TOK + 4]

        rw = {}
        at = [0]

        def rwork(name, n):
            rw[name] = work[:, 1024 + at[0]:1024 + at[0] + n]
            at[0] += n
        for name, n in (("gm", 5), ("eq", 20), ("oh", 20), ("dg", 20), ("eg", 20), ("sg", 5), ("ps", 5), ("E", 80),
                        ("o1", 80), ("o2", 80), ("m1", 5), ("m2", 5), ("d2", 5), ("e2", 5), ("t80", 80), ("f", 5),
                        ("A", 80), ("R", 80), ("nt", 16), ("st", 16), ("b2", 16), ("r", 5), ("bA", 5), ("bB", 5),
                        ("tt", 16), ("cmp", 160), ("tile", 16), ("np", 1), ("io8", 16), ("e128", 16)):
            rwork(name, n)
        assert at[0] <= 1024


        ymem = ([raw[:, n, :] for n in range(RAW)] + [catT_mem[:, n * D:(n + 1) * D] for n in range(TB)]
                + [bc[:, 1, 0, :]])

        def yg(b, j):
            return ymem[2 * b + j]

        block = ctx.enter_context(nc.Block())

        @block.sync
        def _(sp):
            sp.dma_start(x[:, 0:4, :], a["x_sample"].rearrange("b (t p) d -> p (b t) d", p=P)).then_inc(S["x_lat_in"], 16)
            sp.dma_start(x[:, CTX, :], a["x_prompt"][0, :, :]).then_inc(S["x_ctx_in"], 16)
            for q in range(PRE_Q):
                kind, c = pre[q // 4]
                k = 2 * (q % 4)
                if q >= RAW:
                    sp.wait_ge(S["lo"], q - RAW + 1)
                if kind == "conv":
                    for part in range(3):
                        o = 3 * N + part * N + c * P
                        sp.dma_start(raw[:, q % RAW, 0:6 * P].rearrange("p (k a n) -> p k a n", k=2, a=3)[:, :, part, :],
                                     w_in[:, k:k + 2, o:o + P]).then_inc(rawl[q % RAW], 16)
                else:
                    src = {"mod": w_mod, "in": w_in, "o": w_o}[kind]
                    sp.dma_start(raw[:, q % RAW, :].rearrange("p (k n) -> p k n", k=2),
                                 src[:, k:k + 2, c * N:(c + 1) * N]).then_inc(rawl[q % RAW], 16)

            def expert_quarters(tile, j, src, e):
                for r in range(4):
                    out = moe_raw(tile, j, r)
                    n = pos(tile, j, r)
                    if tile[0] is None and RAW <= n < MOE_RAW:
                        sp.wait_ge(S["h2s"], TB)
                    else:
                        back = RAW if tile[0] is None and n < RAW else MOE_RAW
                        v = PRE_Q + n - back + 1
                        sp.wait_ge(S["lo"], v if tile[0] is None else tile[0] * 24 + v)
                    rows = slice(2 * r, 2 * r + 2)
                    if src is w_ed:
                        rows = slice(r, r + 1)
                    else:
                        out = out.rearrange("p (k n) -> p k n", k=2)
                    sp.dma_start(out, src[e, :, rows, :].rearrange("a p k n -> p (a k) n")
                                 ).then_inc(rawl[n % MOE_RAW], 16)

            def rows_in(tile):
                p = tile[1] % 2
                sp.wait_ge(S["xs_tr"], lin(tile, 1, -1))
                at = lin(tile, P, 0)
                src = xs_d[at:at + P, :] if tile[0] is None else xs_d[bass.ds(at, P), :]
                sp.dma_start(xtile[p], src).then_inc(S[f"xs_in{p}"], 16)

            def expert_of(tile):
                if tile[0] is None:
                    return slice(tile[1], tile[1] + 1)
                e = sp.value_load(steer[0:1, bass.ds(lin(tile, 1, 0), 1)], min_val=0, max_val=NEXP - 1)
                return bass.ds(e, 1)

            def tile_in(tile):
                rows_in((tile[0], tile[1] + 1))
                e = expert_of(tile)
                expert_quarters(tile, 0, w_eg, e)
                expert_quarters(tile, 1, w_eu, e)
                expert_quarters(tile, 2, w_ed, expert_of((tile[0], tile[1] - 1)))
            expert_quarters((None, 0), 0, w_eg, slice(0, 1))
            expert_quarters((None, 0), 1, w_eu, slice(0, 1))
            sp.wait_ge(S["scattered"], 16 * 2 * TB)
            sp.dma_start(xtile[0], xs_d[0:P, :]).then_inc(S["xs_in0"], 16)
            sp.dma_start(xtile[1], xs_d[P:2 * P, :]).then_inc(S["xs_in1"], 16)
            tile_in((None, 1))
            sp.wait_ge(S["steer_ready"], 1)
            later = sp.value_load(steer[0:1, 30:31], min_val=NEXP // 2 - 1, max_val=MAX_PAIRS - 1)
            with sp.Fori(0, later) as i:
                tile_in((i, 2))
                tile_in((i, 3))
            expert_quarters((later, 2), 0, w_ed, expert_of((later, 1)))

        @block.gpsimd
        def _(pool):
            pool.memset(ident[:, :], 0.0).then_inc(S["pool_chain"], 1)
            pool.memset(tri[:, :], 1.0).then_inc(S["pool_chain"], 1)
            pool.memset(ones[:, :], 1.0).then_inc(S["consts"], 1)
            pool.memset(epsc, EPS).then_inc(S["consts"], 1)
            pool.memset(col(181), 0.0).then_inc(S["os_out0"], 16)
            pool.memset(col(182), 0.0).then_inc(S["os_out1"], 16)
            pool.wait_ge(S["pool_chain"], 2)
            pool.affine_select(out=ident[:, :], in_=ident[:, :], compare_op=ALU.not_equal, fill=1.0, base=0,
                               pattern=[[-1, P]], channel_multiplier=1).then_inc(S["consts"], 1)
            pool.affine_select(out=tri[:, :], in_=tri[:, :], compare_op=ALU.is_gt, fill=0.0, base=0,
                               pattern=[[1, P]], channel_multiplier=-1).then_inc(S["consts"], 1)
            pool.iota(iota[:, 0:16], pattern=[[1, 16]], base=0, channel_multiplier=0,
                      allow_small_or_imprecise_dtypes=True).then_inc(S["consts"], 1)
            pool.wait_ge(S["roped"], 2 * TB)
            pool.wait_ge(S["qk_tr"], 2 * TB)
            pool.wait_ge(S["cache_out"], 32)
            pool.memset(zero_rows, 0.0).then_inc(S["zero_src"], 1)
            pool.wait_ge(S["zero_src"], 1)
            for t in range(XS_TILES):
                for j in range(2):
                    pool.dma_start(xs_d[t * P:(t + 1) * P, j * 512:(j + 1) * 512], zero_rows).then_inc(S["zeroed"], 16)
            pool.wait_ge(S["zeroed"], 32 * XS_TILES)
            pool.wait_ge(S["slots"], 1)
            for b in range(TB):
                for j in range(2):
                    pool.indirect_dma_start(out=xs_d[:, :], out_offset=bass.IndirectOffsetOnAxis(ap=idx[:, j, b:b + 1], axis=0),
                                            in_=h2[:, b, :], in_offset=None).then_inc(S["scattered"], 16)
            pool.wait_ge(S["steer_ready"], 1)
            pairs = pool.value_load(steer[0:1, 31:32], min_val=NEXP // 2, max_val=MAX_PAIRS)
            pool.wait_ge(S["os_out0"], 16 * pairs + 16)
            pool.wait_ge(S["os_out1"], 16 * pairs + 16)
            pool.tensor_tensor(col(180), epsc, epsc, ALU.add).then_inc(S["pool_chain"], 1)
            pool.wait_ge(S["pool_chain"], 3)
            for b in range(TB):
                for j in range(2):
                    pool.indirect_dma_start(out=yg(b, j), out_offset=None, in_=os_d[:, :],
                                            in_offset=bass.IndirectOffsetOnAxis(ap=idx[:, j, b:b + 1], axis=0)
                                            ).then_inc(gathered[b], 16)

        @block.scalar
        def _(act):
            n_chain = [0]

            def link(ins):
                n_chain[0] += 1
                ins.then_inc(S["act_chain"], 1)
                act.wait_ge(S["act_chain"], n_chain[0])

            with nc.allow_non_contiguous_dma(reason="vectors of the model dimension as columns"):
                act.dma_start(condr[:, 0, :], a["c"].rearrange("b (k p) -> p (b k)", p=P)).then_inc(S["cond_in"], 16)
                act.dma_start(condr[:, 1, :], a["c_ctx"].rearrange("(k p) -> p k", p=P)).then_inc(S["cond_in"], 16)

                def stage_mod(c):
                    brow, grow, _ = mod_mem(c)
                    act.dma_start(brow, a["b_mod"][:, c * N:(c + 1) * N].broadcast_to([2, N])).then_inc(S[f"modst{c % 2}"], 16)
                    if c in norm_of:
                        act.dma_start(grow, a[norm_of[c]][:, (c % 2) * N:(c % 2 + 1) * N].broadcast_to([2, N])).then_inc(S[f"modst{c % 2}"], 16)
                stage_mod(0)
                stage_mod(1)
                act.dma_start(gpre1, a["g_pre1"].rearrange("l (k p) -> p (l k)", p=P)).then_inc(S["gpre_in"], 16)
                for t in range(3):
                    act.dma_start(convw[:, t, :], a["conv_w"][0, t, :].rearrange("(c p) -> p c", p=P)).then_inc(S["convw_in"], 16)
                act.dma_start(subg, a["subln_g"].rearrange("l p -> p l")).then_inc(S["subg_in"], 16)
                for v, n in enumerate(("lambda_q1", "lambda_k1", "lambda_q2", "lambda_k2")):
                    act.dma_start(lamv[:, v, :], a[n].broadcast_to([P, DQ])).then_inc(S["lam_in"], 16)
                for t in range(2):
                    act.dma_start(rope[:, :, t, :], a["rope"][t, :, :].rearrange("(t p) d -> p t d", p=P)).then_inc(S["rope_in"], 16)
                act.dma_start(wr[:, :, 0:GROUPS], a["w_router_group"].rearrange("l (k p) n -> p (l k) n", p=P)).then_inc(S["wr_in"], 16)
                act.dma_start(wr[:, :, GROUPS:], a["w_router_expert"].rearrange("l (k p) n -> p (l k) n", p=P)).then_inc(S["wr_in"], 16)
                act.dma_start(ck, a["cache_k"].rearrange("b l h p d -> p (b l h) d")).then_inc(S["ck_in"], 16)
            act.wait_ge(S["cond_in"], 32)
            nc.scalar.activation(condc.rearrange("p k c -> p c k"), condr, ACT.Silu).then_inc(S["silu_done"], 1)
            act.wait_ge(S["silu_done"], 1)
            nc.scalar.copy(conds[:, 0, :, :], condc).then_inc(S["conds_hi"], 1)

            def split_panel(n):
                m = 6 * P if pre[n][0] == "conv" else QUARTER
                for q in range(4 * n, 4 * n + 4):
                    act.wait_ge(rawl[q % RAW], raw_value[q])
                    if n >= 2 and q == 4 * n:
                        used(act, n - 2)
                    nc.scalar.copy(spl[:, q % SPLIT, 0, 0:m], raw[:, q % RAW, 0:m]).then_inc(S["hi"], 1)
            act.wait_ge(S["x_lat_in"], 16)
            act.wait_ge(S["x_ctx_in"], 16)
            act.wait_ge(S["consts"], 5)
            for b in range(TB):
                ins = nc.scalar.activation(xn[:, b, :], x[:, b, :], ACT.Square, accum_out=ssq[:, b:b + 1])
            link(ins)
            nc.scalar.activation(rt, ssq, ACT.Sqrt, bias=epsc, scale=1.0 / D).then_inc(S["rms1"], 1)
            act.wait_ge(S["lam_prod"], 1)
            nc.scalar.activation(lamw[:, 2:4], lamw[:, 0:2], ACT.Exp).then_inc(S["lam_exp"], 1)
            split_panel(0)
            split_panel(1)
            for c in range(2, MOD_EARLY):
                act.wait_ge(S["mod_row"], c - 1)
                act.wait_ge(S["col_mm"], c - 1)
                stage_mod(c)
                split_panel(c)
            split_panel(4)
            act.wait_ge(S["a1_ready"], 1)
            for k in range(KC):
                act.wait_ge(S["h_tr"], k + 1)
                if k >= 2:
                    act.wait_ge(S["hT_ctx"], k - 1)
                hf = work[:, TOK * (k % 2):TOK * (k % 2 + 1)]
                nc.scalar.activation(hf[:, 0:L_LAT], ps[:, 2 * (k % 2), :], ACT.Identity,
                                     bias=B1[:, 0, k:k + 1], scale=A1[:, 0, k:k + 1]).then_inc(S["hf_lat"], 1)
                act.wait_ge(S["hf_lat"], k + 1)
                act.wait_ge(S["hf_ctx"], k + 1)
                nc.scalar.copy(hS[:, 0, k, :], hf).then_inc(S["hT_lat"], 1)
            split_panel(5)
            act.wait_ge(S["h_tr"], KC)
            act.dma_start(V[:, 0, :].rearrange("p (h d) -> p h d", h=H), a["cache_v"].rearrange("b l h p d -> p (b l h) d")).then_inc(S["cv_in"], 16)
            def qk_out(g):
                part, b = g // TB, g % TB
                act.wait_ge(S["qk_tr"], g + 1)
                dst = qT[:, :, b * P:(b + 1) * P] if part == 0 else kT[:, :, (b + 1) * P:(b + 2) * P]
                nc.scalar.copy(dst, ps[:, 2 + g % 2, :].rearrange("p (h t) -> p h t", h=H)).then_inc(S["qkT"], 1)
            for g in range(2 * TB):
                qk_out(g)
                if g == TB:
                    split_panel(6)
            for b in range(TB):
                act.wait_ge(S["z_mm"], 2 * TB + b + 1)
                nc.scalar.copy(V[:, b + 1, :], ps[:, (2 * TB + b) % 2, :]).then_inc(S["v_done"], 1)
                if b == 0:
                    split_panel(7)
            act.wait_ge(S["v_done"], TB)
            act.dma_start(a["out_v"].rearrange("b l h p d -> p (b l h) d"), V[:, TB, :].rearrange("p (h d) -> p h d", h=H)).then_inc(S["cache_out"], 16)
            act.wait_ge(S["roped"], 2 * TB)
            act.dma_start(a["out_k"].rearrange("b l h p d -> p (b l h) d"), qr(2 * TB - 1).rearrange("p (h d) -> p h d", h=H)).then_inc(S["cache_out"], 16)
            act.wait_ge(S["qk_tr"], 2 * TB + 1)
            nc.scalar.copy(kT[:, :, 0:P], ps[:, 6, :].rearrange("p (h t) -> p h t", h=H)).then_inc(S["qkT"], 1)
            def exps(u):
                h, b = UNITS[u]
                nk = KEYS if b < CTX else L_CTX
                for c in range(2):
                    act.wait_ge(S["neg_max"], 2 * u + c + 1)
                    if u >= 1 and c == 0:
                        act.wait_ge(S["p_ready"], u)
                    nc.scalar.activation(e_buf(u, c)[:, 0:nk], psf[:, 1024 * c:1024 * c + nk], ACT.Exp,
                                         bias=nm[:, u % 2, c:c + 1], scale=SCALE,
                                         accum_out=sm[:, u % 2, c:c + 1]).then_inc(S[f"exp{c}"], 1)

            def pt_out(u):
                act.wait_ge(S["p_tr"], u + 1)
                if u >= 1:
                    act.wait_ge(S["pv_mm"], u)
                nk = N if UNITS[u][1] < CTX else L_CTX
                nc.scalar.copy(pt_buf(u)[:, 0:nk], ps[:, 4, 0:nk]).then_inc(S["pt_act"], 1)

            def o_out(u):
                h, b = UNITS[u]
                act.wait_ge(S["pv_mm"], u + 1)
                nc.scalar.copy(catT[:, h, b * P:(b + 1) * P], ps[:, 5, P:2 * P]).then_inc(S["o_evac"], 1)

            def head_root(h):
                act.wait_ge(S["osq_mm"], h + 1)
                nc.scalar.activation(osq_buf, psf[:, 3072:3072 + TOK], ACT.Sqrt, bias=epsc, scale=1.0 / DV).then_inc(S["osr"], 1)

            def conv_part(g):
                if g % 3 == 0:
                    act.wait_ge(S["conv_mm"], g + 1)
                    if g == 0:
                        act.wait_ge(S["qk_tr"], 2 * TB)
                        act.wait_ge(S["cache_out"], 32)
                    else:
                        act.wait_ge(S["conv_u"], 2 * (g // 3))
                    nc.scalar.copy(Cst[:, 0:L_LAT], ps[:, 6, :]).then_inc(S["conv_c"], 1)
                    nc.scalar.copy(Cst[:, L_LAT:TOK], ps[:, 7, 0:P]).then_inc(S["conv_c"], 1)
                    split_panel(8 + g // 3)

            def send_mod(c):
                act.wait_ge(S["mod_row"], c + 1)
                act.dma_start(mod_d[:, c * N:(c + 1) * N], mod_mem(c)[2]).then_inc(S[f"modout{c % 2}"], 16)

            def split_cat(k):
                act.wait_ge(*(cat_ready(k)))
                nc.scalar.copy(hS[:, 0, k, :], catT[:, k, :]).then_inc(S["cat_hi"], 1)
            for u in range(len(UNITS)):
                if u >= 1:
                    pt_out(u - 1)
                if u in ROOT_STEP:
                    head_root(ROOT_STEP[u])
                exps(u)
                if u >= 1:
                    o_out(u - 1)
                if u < 12:
                    conv_part(u)
                else:
                    c = u - 12 + MOD_EARLY
                    if u == 12:
                        act.wait_ge(S["conv_y"], 8)
                        stage_mod(c)
                        stage_mod(c + 1)
                    split_cat(CAT_ORDER[u - 12]) if u - 12 < 7 else None
                    split_panel(place["mod", c] + 1)
                    send_mod(c)
                    if c + 2 < N_MOD:
                        stage_mod(c + 2)
            pt_out(len(UNITS) - 1)
            o_out(len(UNITS) - 1)
            head_root(H - 1)
            split_panel(place["o", 1])
            split_cat(H - 1)
            act.wait_ge(S["modout0"], 16 * (N_MOD - MOD_EARLY) // 2)
            act.wait_ge(S["modout1"], 16 * (N_MOD - MOD_EARLY) // 2)
            for v, off in enumerate((2 * D, 3 * D, 4 * D, 5 * D)):
                for c in range(2):
                    act.dma_start(bc[:, v, c, :], mod_d[c:c + 1, off:off + D].broadcast_to([P, D])).then_inc(S[f"bc{2 * v + c}"], 16)
            act.dma_start(x[:, 0:4, :], a["x_sample"].rearrange("b (t p) d -> p (b t) d", p=P)).then_inc(S["x_again"], 16)
            act.dma_start(x[:, CTX, :], a["x_prompt"][0, :, :]).then_inc(S["x_again"], 16)
            act.wait_ge(S["cat_lo"], KC)
            for b in range(TB):
                act.wait_ge(S["wo_mm"], b + 1)
                link(nc.scalar.activation(h2[:, b, :], psf[:, 1024 * (b % 2):1024 * (b % 2) + D], ACT.Square, accum_out=ss2[:, b:b + 1]))
                nc.scalar.activation(rt2[:, b:b + 1], ss2[:, b:b + 1], ACT.Sqrt, bias=epsc, scale=1.0 / D).then_inc(S["rt2s"], 1)
                act.wait_ge(S["x2s"], b + 1)
                link(nc.scalar.activation(h2[:, b, :], x[:, b, :], ACT.Square, accum_out=ss3[:, b:b + 1]))
                nc.scalar.activation(rt3[:, b:b + 1], ss3[:, b:b + 1], ACT.Sqrt, bias=epsc, scale=1.0 / D).then_inc(S["rt3s"], 1)
                act.wait_ge(S["h2_tr"], b + 1)
                if b >= 1:
                    act.wait_ge(S["lg_mm"], b)
                nc.scalar.copy(work[:, 0:1024], psf[:, 2048:3072]).then_inc(S["h2T_ev"], 1)
            def split_expert(tile, j):
                for r in range(4):
                    if tile[0] is None and tile[1] == 0:
                        act.wait_ge(S["wo_mm"], TB)
                    elif tile[0] is None and j < 2:
                        act.wait_ge(S[("g_mm", "u_mm")[j]], r + 1)
                    else:
                        act.wait_ge(S[("u_mm", "dn_mm", "g_mm")[j]], lin(tile, 4, (-3, -7, 1)[j] + r))
                    act.wait_ge(rawl[pos(tile, j, r) % MOE_RAW], moe_loaded(tile, j, r))
                    nc.scalar.copy(spl[:, moe_split_slot(tile, j, r), 0, :], moe_raw(tile, j, r)).then_inc(S["hi"], 1)
            split_expert((None, 0), 0)
            act.wait_ge(S["oh_ready"], 1)
            nc.scalar.activation(rw["eg"], rw["dg"], ACT.Exp).then_inc(S["exp0"], 1)
            nc.scalar.activation(rw["e2"], rw["d2"], ACT.Exp).then_inc(S["exp0"], 1)
            split_expert((None, 0), 1)

            def xT_hi(tile):
                act.wait_ge(S["xs_tr"], lin(tile, 1, 1))
                for b in range(2):
                    nc.scalar.copy(hs[:, 0, b * N:(b + 1) * N], ps[:, 2 + b, :]).then_inc(S["xT_act"], 1)

            def aT_hi(tile):
                act.wait_ge(S["a_tr"], lin(tile, 1, 1))
                nc.scalar.copy(hs[:, 0, 1024:1536], ps[:, 4, :]).then_inc(S["aT_ev"], 1)

            def out_rows(tile):
                p = tile[1] % 2
                act.wait_ge(S["dn_mm"], lin(tile, 4, 4))
                i, c = tile
                act.wait_ge(S[f"os_out{p}"], 16 * (c // 2) + 16 if i is None else 16 * i + (16 * (c // 2) + 16))
                nc.scalar.copy(ostage[p], psf[:, 2560:3584]).then_inc(S["o_act"], 1)
                act.wait_ge(S["o_act"], lin(tile, 1, 1))
                at = lin(tile, P, 0)
                dst = os_d[at:at + P, :] if i is None else os_d[bass.ds(at, P), :]
                act.dma_start(dst, ostage[p]).then_inc(S[f"os_out{p}"], 16)

            def gate_act(tile):
                act.wait_ge(S["g_mm"], lin(tile, 4, 4))
                if tile[0] is not None or tile[1] > 0:
                    act.wait_ge(S["act_a"], lin(tile, 1, 0))
                nc.scalar.activation(sil, ps[:, 0, :], ACT.Silu).then_inc(S["sil"], 1)

            def expert_tile(tile):
                split_expert(tile, 0)
                aT_hi((tile[0], tile[1] - 1))
                if tile[0] is not None:
                    out_rows((tile[0], tile[1] - 2))
                split_expert(tile, 1)
                gate_act(tile)
                split_expert(tile, 2)
                xT_hi((tile[0], tile[1] + 1))
            act.wait_ge(S["steer_ready"], 1)
            xT_hi((None, 0))
            gate_act((None, 0))
            xT_hi((None, 1))
            expert_tile((None, 1))
            later = act.value_load(steer[0:1, 30:31], min_val=NEXP // 2 - 1, max_val=MAX_PAIRS - 1)
            with act.Fori(0, later) as i:
                expert_tile((i, 2))
                expert_tile((i, 3))
            split_expert((later, 2), 0)
            aT_hi((later, 1))
            out_rows((later, 0))
            out_rows((later, 1))
            for b in range(TB):
                act.wait_ge(S["ysq"], b + 1)
                link(nc.scalar.activation(yg(b, 1), yg(b, 0), ACT.Square, accum_out=ss4[:, b:b + 1]))
                nc.scalar.activation(rt4[:, b:b + 1], ss4[:, b:b + 1], ACT.Sqrt, bias=epsc, scale=1.0 / D).then_inc(S["yrt"], 1)
            for b in range(TB):
                act.wait_ge(S["yout"], b + 1)
                dst = a["out_lat"][0, b * P:(b + 1) * P, :] if b < CTX else a["out_ctx"][0, :, :]
                act.dma_start(dst, yg(b, 1)).then_inc(S["y_dma"], 16)
            act.wait_ge(S["y_dma"], 16 * TB)
            act.wait_ge(S["cache_out"], 32)

        @block.vector
        def _(dve):
            n_chain = [0]

            def link(ins):
                n_chain[0] += 1
                ins.then_inc(S["dve_chain"], 1)
                dve.wait_ge(S["dve_chain"], n_chain[0])

            tt, ts, stt = nc.vector.tensor_tensor, nc.vector.tensor_scalar, nc.vector.scalar_tensor_tensor
            dve.wait_ge(S["lam_in"], 64)
            link(tt(lamp, lamv[:, 0:4:2, :], lamv[:, 1:4:2, :], ALU.mult))
            nc.vector.reduce_sum(lamw[:, 0:2], lamp, axis=AX).then_inc(S["lam_prod"], 1)
            dve.wait_ge(S["rms1"], 1)
            link(nc.vector.reciprocal(rstd, rt))
            for b in range(TB):
                ts(xn[:, b, :], x[:, b, :], rstd[:, b:b + 1], None, ALU.mult).then_inc(S["xn_ready"], 1)
            dve.wait_ge(S["lam_exp"], 1)
            link(tt(nlam, lamw[:, 3:4], lamw[:, 2:3], ALU.subtract))
            link(ts(nlam, nlam, -LAM_INIT, None, ALU.add))

            def split_lo(slot, rslot, m, q):
                dve.wait_ge(S["hi"], q)
                tt(spl[:, slot, 1, 0:m], raw[:, rslot, 0:m], spl[:, slot, 0, 0:m].bitcast(F32), ALU.subtract).then_inc(S["lo"], 1)

            def split_panel(n):
                for q in range(4 * n, 4 * n + 4):
                    split_lo(q % SPLIT, q % RAW, 6 * P if pre[n][0] == "conv" else QUARTER, q + 1)
            dve.wait_ge(S["conds_hi"], 1)
            tt(conds[:, 1, :, :], condc, conds[:, 0, :, :].bitcast(F32), ALU.subtract).then_inc(S["conds_lo"], 1)

            def mod_row(c):
                brow, grow, row = mod_mem(c)
                dve.wait_ge(S["mod_mm"], c + 1)
                dve.wait_ge(S[f"modst{c % 2}"], MODST[c])
                if 2 <= c < MOD_EARLY:
                    dve.wait_ge(S["col_mm"], c - 1)
                if c >= MOD_EARLY + 2:
                    dve.wait_ge(S[f"modout{c % 2}"], 16 * ((c - MOD_EARLY) // 2))
                src = ps[0:2, (4 if c < MOD_EARLY else 6) + c % 2, :]
                if c in norm_of:
                    link(tt(row, src, brow, ALU.add))
                    one = 1.0 if c in (8, 9) else 0.0
                    stt(row, row, one, grow, ALU.add, ALU.mult).then_inc(S["mod_row"], 1)
                else:
                    tt(row, src, brow, ALU.add).then_inc(S["mod_row"], 1)
            split_panel(0)
            split_panel(1)
            for c in range(MOD_EARLY):
                mod_row(c)
                if c + 2 < MOD_EARLY:
                    split_panel(c + 2)
            split_panel(4)
            dve.wait_ge(S["gpre_in"], 16)
            dve.wait_ge(S["col_mm"], MOD_EARLY)
            cols = ps[:, 6, 0:32].rearrange("p (s k c) -> p s c k", s=2, c=2)
            link(nc.vector.tensor_copy(B1, cols[:, 0, :, :]))
            link(stt(A1[:, 0, :], cols[:, 1, 0, :], 1.0, gpre1, ALU.add, ALU.mult))
            stt(A1[:, 1, :], cols[:, 1, 1, :], 1.0, gpre1, ALU.add, ALU.mult).then_inc(S["a1_ready"], 1)
            dve.wait_ge(S["a1_ready"], 1)
            for k in range(KC):
                dve.wait_ge(S["h_tr"], k + 1)
                hf = work[:, TOK * (k % 2):TOK * (k % 2 + 1)]
                if k >= 2:
                    dve.wait_ge(S["hT_ctx"], k - 1)
                ts(hf[:, L_LAT:TOK], ps[:, 2 * (k % 2) + 1, 0:P], A1[:, 1, k:k + 1], B1[:, 1, k:k + 1],
                   ALU.mult, ALU.add).then_inc(S["hf_ctx"], 1)
                dve.wait_ge(S["hT_lat"], k + 1)
                tt(hS[:, 1, k, :], hf, hS[:, 0, k, :].bitcast(F32), ALU.subtract).then_inc(S["hT_ctx"], 1)
            split_panel(5)
            dve.wait_ge(S["hT_ctx"], KC)
            dve.wait_ge(S["rope_in"], 32)
            for g in range(2 * TB):
                b = g % TB
                src = ps[:, g % 2, :]
                dve.wait_ge(S["z_mm"], g + 1)
                if g >= 2:
                    dve.wait_ge(S["qk_tr"], g - 1)
                if b == CTX:
                    nc.vector.tensor_copy(qr(g), src).then_inc(S["roped"], 1)
                    continue
                if g == TB + 1:
                    split_panel(6)
                if g >= 1:
                    dve.wait_ge(S["roped"], g)
                t1 = work[:, 0:512]
                t2 = work[:, 512:1024]
                cos = rope[:, b, 0:1, :].broadcast_to([P, 8, DQ])
                sin = rope[:, b, 1, :].rearrange("p (a s d) -> p a s d", a=2, s=2)
                tt(t1.rearrange("p (g d) -> p g d", g=8), src.rearrange("p (g d) -> p g d", g=8), cos, ALU.mult).then_inc(S["dve_chain"], 1)
                n_chain[0] += 1
                sv = src.rearrange("p (g a s d) -> p g a s d", g=8, a=2, s=2)
                tv = t2.rearrange("p (g a s d) -> p g a s d", g=8, a=2, s=2)
                for s in range(2):
                    sn = sin[:, :, s, :].rearrange("p (o a) d -> p o a d", o=1).broadcast_to([P, 8, 2, 16])
                    ins = tt(tv[:, :, :, s, :], sv[:, :, :, 1 - s, :], sn, ALU.mult)
                    if s == 0:
                        ins.then_inc(S["dve_chain"], 1)
                        n_chain[0] += 1
                link(ins)
                tt(qr(g), t1, t2, ALU.add).then_inc(S["roped"], 1)
            split_panel(7)
            dve.wait_ge(S["convw_in"], 48)
            dve.wait_ge(S["qk_tr"], 2 * TB)
            dve.wait_ge(S["cache_out"], 32)
            for edge in (CUl[:, 0:1], CUl[:, L_LAT + 1:L_LAT + 2], CUc[:, 0:1], CUc[:, L_CTX + 1:L_CTX + 2]):
                link(nc.vector.memset(edge, 0.0))

            def conv_part(g):
                cb = g // 3
                if g % 3 == 0:
                    split_panel(8 + cb)
                    return
                dve.wait_ge(S["conv_mm"], g + 1)
                y = [catT[:, 4 + cb, 0:L_LAT], catT[:, 4 + cb, L_LAT:TOK]]
                if g % 3 == 1:
                    dve.wait_ge(S["conv_c"], 2 * cb + 2)
                    tt(CUl[:, 1:L_LAT + 1], ps[:, 6, :], Cst[:, 0:L_LAT], ALU.mult).then_inc(S["conv_u"], 1)
                    tt(CUc[:, 1:L_CTX + 1], ps[:, 7, 0:P], Cst[:, L_LAT:TOK], ALU.mult).then_inc(S["conv_u"], 1)
                    dve.wait_ge(S["conv_u"], 2 * cb + 2)
                    for n, (buf, ln) in enumerate(((CUl, L_LAT), (CUc, L_CTX))):
                        link(ts(y[n], buf[:, 0:ln], convw[:, 0, cb:cb + 1], None, ALU.mult))
                        link(stt(y[n], buf[:, 1:ln + 1], convw[:, 1, cb:cb + 1], y[n], ALU.mult, ALU.add))
                        link(stt(y[n], buf[:, 2:ln + 2], convw[:, 2, cb:cb + 1], y[n], ALU.mult, ALU.add))
                else:
                    tt(y[0], ps[:, 6, :], y[0], ALU.mult).then_inc(S["conv_y"], 1)
                    tt(y[1], ps[:, 7, 0:P], y[1], ALU.mult).then_inc(S["conv_y"], 1)

            def maxes(u):
                nk = KEYS if UNITS[u][1] < CTX else L_CTX
                for c in range(2):
                    dve.wait_ge(S["s_mm"], 2 * u + c + 1)
                    link(nc.vector.reduce_max(mx[:, u % 2, c:c + 1], psf[:, 1024 * c:1024 * c + nk], axis=AX))
                    ts(nm[:, u % 2, c:c + 1], mx[:, u % 2, c:c + 1], -SCALE, None, ALU.mult).then_inc(S["neg_max"], 1)

            def combine(u):
                nk = KEYS if UNITS[u][1] < CTX else L_CTX
                dve.wait_ge(S["exp0"], u + 1)
                dve.wait_ge(S["exp1"], u + 1)
                link(nc.vector.reciprocal(rc[:, u % 2, :], sm[:, u % 2, :]))
                link(tt(nr2[:, u % 2:u % 2 + 1], rc[:, u % 2, 1:2], nlam, ALU.mult))
                e2 = e_buf(u, 1)[:, 0:nk]
                link(ts(e2, e2, nr2[:, u % 2:u % 2 + 1], None, ALU.mult))
                if u >= 1:
                    dve.wait_ge(S["p_tr"], u)
                stt(p_buf(u)[:, 0:nk], e_buf(u, 0)[:, 0:nk], rc[:, u % 2, 0:1], e2, ALU.mult, ALU.add).then_inc(S["p_ready"], 1)

            def pt_out(u):
                if UNITS[u][1] == CTX:
                    return
                dve.wait_ge(S["p_tr"], u + 1)
                if u >= 1:
                    dve.wait_ge(S["pv_mm"], u)
                nc.vector.tensor_copy(pt_buf(u)[:, N:KEYS], ps[:, 5, 0:P]).then_inc(S["pt_dve"], 1)

            def head_square(h):
                dve.wait_ge(S["o_evac"], TB * (h + 1))
                if h >= 1:
                    dve.wait_ge(S["onorm"], h)
                tt(osq_buf, catT[:, h, :], catT[:, h, :], ALU.mult).then_inc(S["osq"], 1)

            def head_norm(h):
                dve.wait_ge(S["osr"], h + 1)
                link(nc.vector.reciprocal(osq_buf, osq_buf))
                link(stt(catT[:, h, :], catT[:, h, :], subg, osq_buf, ALU.mult, ALU.mult))
                ts(catT[:, h, :], catT[:, h, :], 1.0 - LAM_INIT, None, ALU.mult).then_inc(S["onorm"], 1)

            def split_cat(n):
                k = CAT_ORDER[n]
                dve.wait_ge(S["cat_hi"], n + 1)
                tt(hS[:, 1, k, :], catT[:, k, :], hS[:, 0, k, :].bitcast(F32), ALU.subtract).then_inc(S["cat_lo"], 1)
            dve.wait_ge(S["subg_in"], 16)
            for u in range(len(UNITS)):
                if u >= 1:
                    pt_out(u - 1)
                maxes(u)
                combine(u)
                if u + 1 in ROOT_STEP:
                    head_square(ROOT_STEP[u + 1])
                if u in ROOT_STEP:
                    head_norm(ROOT_STEP[u])
                if u < 12:
                    conv_part(u)
                else:
                    c = u - 12 + MOD_EARLY
                    if u - 12 < 7:
                        split_cat(u - 12)
                    split_panel(place["mod", c] + 1)
                    mod_row(c)
            pt_out(len(UNITS) - 1)
            head_square(H - 1)
            head_norm(H - 1)
            split_panel(place["o", 1])
            split_cat(KC - 1)
            dve.wait_ge(S["x_again"], 32)
            dve.wait_ge(S["zeroed"], 32 * XS_TILES)
            for b in range(TB):
                c = 1 if b == CTX else 0
                t = work[:, 1024:2048]
                if c == 1 or b == 0:
                    for v in range(4):
                        dve.wait_ge(S[f"bc{2 * v + c}"], 16)
                dve.wait_ge(S["rt2s"], b + 1)
                link(nc.vector.reciprocal(rs2[:, b:b + 1], rt2[:, b:b + 1]))
                link(stt(t, psf[:, 1024 * (b % 2):1024 * (b % 2) + D], rs2[:, b:b + 1], bc[:, 0, c, :], ALU.mult, ALU.mult))
                tt(x[:, b, :], x[:, b, :], t, ALU.add).then_inc(S["x2s"], 1)
                dve.wait_ge(S["rt3s"], b + 1)
                link(nc.vector.reciprocal(rs3[:, b:b + 1], rt3[:, b:b + 1]))
                link(stt(h2[:, b, :], x[:, b, :], rs3[:, b:b + 1], bc[:, 2, c, :], ALU.mult, ALU.mult))
                tt(h2[:, b, :], h2[:, b, :], bc[:, 1, c, :], ALU.add).then_inc(S["h2s"], 1)
            def split_lo_moe(tile, j):
                for r in range(4):
                    dve.wait_ge(S["hi"], moe_lo(tile, j, r))
                    slot = moe_split_slot(tile, j, r)
                    tt(spl[:, slot, 1, :], moe_raw(tile, j, r), spl[:, slot, 0, :].bitcast(F32), ALU.subtract).then_inc(S["lo"], 1)
            split_lo_moe((None, 0), 0)
            dve.wait_ge(S["lg_mm"], TB)
            dve.wait_ge(S["consts"], 5)
            link(nc.vector.tensor_copy(logit[:, :, :], ps[:, 6, 0:TB * 20].rearrange("p (b n) -> p b n", b=TB)))
            v3 = lambda name, b=TB: rw[name].rearrange("p (b n) -> p b n", b=b)
            bcast = lambda ap, n: ap.rearrange("p (b o) -> p b o", o=1).broadcast_to([P, TB, n])
            G, E16 = logit[:, :, 0:GROUPS], logit[:, :, GROUPS:]
            link(ts(rw["io8"], iota[:, 0:16], -1.0, 16.0, ALU.mult, ALU.add))
            link(ts(rw["e128"], iota[:, 0:16], float(P), None, ALU.mult))

            def first_max(out, vals, m, n):
                io = rw["io8"][:, 0:n].rearrange("p (o n) -> p o n", o=1).broadcast_to([P, TB, n])
                link(nc.vector.reduce_max(m, vals, axis=AX))
                link(tt(out, vals, bcast(m, n), ALU.is_equal))
                link(tt(out, out, io, ALU.mult))
                link(nc.vector.reduce_max(rw["f"], out, axis=AX))
                link(tt(out, out, bcast(rw["f"], n), ALU.is_equal))
            first_max(v3("oh"), G, rw["gm"], GROUPS)
            link(tt(v3("dg"), G, bcast(rw["gm"], GROUPS), ALU.subtract))
            oh4 = rw["oh"].rearrange("p (b g o) -> p b g o", b=TB, o=1).broadcast_to([P, TB, GROUPS, EPG])
            v4 = lambda ap: ap.rearrange("p b (g e) -> p b g e", g=GROUPS)
            link(tt(v4(v3("E")), v4(E16), oh4, ALU.mult))
            link(ts(v4(v3("t80")), oh4, -1.0, BIG, ALU.add, ALU.mult))
            link(tt(v3("E"), v3("E"), v3("t80"), ALU.add))
            first_max(v3("o1"), v3("E"), rw["m1"], NEXP)
            link(stt(v3("E"), v3("o1"), -4 * BIG, v3("E"), ALU.mult, ALU.add))
            first_max(v3("o2"), v3("E"), rw["m2"], NEXP)
            link(tt(v3("A"), v3("o1"), v3("o2"), ALU.add))
            tt(rw["d2"], rw["m2"], rw["m1"], ALU.subtract).then_inc(S["oh_ready"], 1)
            dve.wait_ge(S["exp0"], len(UNITS) + 2)
            link(nc.vector.reduce_sum(rw["sg"], v3("eg"), axis=AX))
            link(nc.vector.reciprocal(rw["ps"], rw["sg"]))
            link(ts(rw["m1"], rw["e2"], 1.0, None, ALU.add))
            link(nc.vector.reciprocal(rw["m2"], rw["m1"]))
            link(tt(gate[:, 0, :], rw["m2"], rw["ps"], ALU.mult))
            link(tt(gate[:, 1, :], gate[:, 0, :], rw["e2"], ALU.mult))
            dve.wait_ge(S["cum_mm"], 1)
            link(nc.vector.tensor_copy(v3("R"), ps[:, 7, 0:TB * 16].rearrange("p (b n) -> p b n", b=TB)))
            cntp = ps[:, 7, 80:96]
            link(ts(rw["nt"], cntp, float(P), None, ALU.is_gt))
            for j in range(2, 5):
                link(stt(rw["nt"], cntp, float(P * j), rw["nt"], ALU.is_gt, ALU.add))
            link(nc.vector.tensor_tensor_scan(rw["st"], ones[:, 0:16], rw["nt"], 0.0, ALU.mult, ALU.add))
            link(tt(rw["b2"], rw["st"], rw["nt"], ALU.subtract))
            link(ts(rw["b2"], rw["b2"], float(NEXP - 1), float(P), ALU.add, ALU.mult))
            for j, o in enumerate(("o1", "o2")):
                for out, w in (("r", v3("R")), ("bA", rw["e128"].rearrange("p (o n) -> p o n", o=1).broadcast_to([P, TB, 16])),
                               ("bB", rw["b2"].rearrange("p (o n) -> p o n", o=1).broadcast_to([P, TB, 16]))):
                    link(tt(v3("t80"), v3(o), w, ALU.mult))
                    link(nc.vector.reduce_sum(rw[out], v3("t80"), axis=AX))
                link(tt(rw["bB"], rw["bB"], rw["bA"], ALU.subtract))
                link(stt(rw["bB"], rw["r"], float(P), rw["bB"], ALU.is_ge, ALU.mult))
                link(tt(rw["bA"], rw["bA"], rw["bB"], ALU.add))
                link(tt(rw["r"], rw["r"], rw["bA"], ALU.add))
                link(nc.vector.tensor_copy(idx[:, j, :], rw["r"]))
            dve.wait_ge(S["h2s"], TB)
            nc.vector.tensor_copy(rw["np"], rw["gm"][:, 0:1]).then_inc(S["slots"], 1)
            cmp = rw["cmp"][0:1, :].rearrange("p (t e) -> p t e", t=10)
            link(tt(cmp, rw["st"][0:1, :].rearrange("p (o e) -> p o e", o=1).broadcast_to([1, 10, 16]),
                    iota[0:1, 0:10].rearrange("p (t o) -> p t o", o=1).broadcast_to([1, 10, 16]), ALU.is_le))
            link(nc.vector.reduce_sum(rw["tt"][0:1, 0:10], cmp, axis=AX))
            link(ts(rw["tt"][0:1, 0:10], rw["tt"][0:1, 0:10], float(NEXP - 1), None, ALU.min))
            link(nc.vector.memset(steer[:, :], 0))
            link(nc.vector.tensor_copy(steer[0:1, 16:26], rw["tt"][0:1, 0:10]))
            link(nc.vector.tensor_copy(steer[0:1, 0:16], iota[0:1, 0:16]))
            link(ts(rw["tile"][0:1, 0:5], iota[0:1, 0:5], 2.0, None, ALU.mult))
            link(tt(rw["tile"][0:1, 8:13], rw["st"][0:1, 15:16].broadcast_to([1, 5]), rw["tile"][0:1, 0:5], ALU.is_gt))
            link(nc.vector.reduce_sum(rw["np"][0:1, :], rw["tile"][0:1, 8:13], axis=AX))
            link(ts(rw["np"][0:1, :], rw["np"][0:1, :], float(NEXP // 2), None, ALU.add))
            link(nc.vector.tensor_copy(steer[0:1, 31:32], rw["np"][0:1, :]))
            link(ts(steer[0:1, 30:31], rw["np"][0:1, :], -1.0, None, ALU.add))
            nc.vector.tensor_copy(rw["np"], rw["gm"][:, 0:1]).then_inc(S["steer_ready"], 1)
            def xT_lo(tile):
                for b in range(2):
                    dve.wait_ge(S["xT_act"], lin(tile, 2, b + 1))
                    tt(hs[:, 1, b * N:(b + 1) * N], ps[:, 2 + b, :], hs[:, 0, b * N:(b + 1) * N].bitcast(F32),
                       ALU.subtract).then_inc(S["xT_lo"], 1)

            def aT_lo(tile):
                dve.wait_ge(S["aT_ev"], lin(tile, 1, 1))
                tt(hs[:, 1, 1024:1536], ps[:, 4, :], hs[:, 0, 1024:1536].bitcast(F32), ALU.subtract).then_inc(S["aT_lo"], 1)

            def gated(tile):
                dve.wait_ge(S["sil"], lin(tile, 1, 1))
                dve.wait_ge(S["u_mm"], lin(tile, 4, 4))
                if tile[0] is not None or tile[1] > 0:
                    dve.wait_ge(S["a_tr"], lin(tile, 1, 0))
                tt(act_rows, ps[:, 1, :], sil, ALU.mult).then_inc(S["act_a"], 1)

            def expert_tile(tile):
                split_lo_moe(tile, 0)
                aT_lo((tile[0], tile[1] - 1))
                split_lo_moe(tile, 1)
                split_lo_moe(tile, 2)
                gated(tile)
                xT_lo((tile[0], tile[1] + 1))
            split_lo_moe((None, 0), 1)
            dve.wait_ge(S["steer_ready"], 1)
            xT_lo((None, 0))
            gated((None, 0))
            xT_lo((None, 1))
            expert_tile((None, 1))
            later = dve.value_load(steer[0:1, 30:31], min_val=NEXP // 2 - 1, max_val=MAX_PAIRS - 1)
            with dve.Fori(0, later) as i:
                expert_tile((i, 2))
                expert_tile((i, 3))
            split_lo_moe((later, 2), 0)
            aT_lo((later, 1))
            for b in range(TB):
                dve.wait_ge(gathered[b], 32)
                link(ts(yg(b, 1), yg(b, 1), gate[:, 1, b:b + 1], None, ALU.mult))
                stt(yg(b, 0), yg(b, 0), gate[:, 0, b:b + 1], yg(b, 1), ALU.mult, ALU.add).then_inc(S["ysq"], 1)
            for b in range(TB):
                c = 1 if b == CTX else 0
                dve.wait_ge(S["yrt"], b + 1)
                link(nc.vector.reciprocal(rs4[:, b:b + 1], rt4[:, b:b + 1]))
                link(stt(yg(b, 0), yg(b, 0), rs4[:, b:b + 1], bc[:, 3, c, :], ALU.mult, ALU.mult))
                tt(yg(b, 1), yg(b, 0), x[:, b, :], ALU.add).then_inc(S["yout"], 1)

        @block.tensor
        def _(pe):
            mm = nc.tensor.matmul

            def part_ready(n, k):
                if k % 2 == 0:
                    pe.wait_ge(S["lo"], 4 * n + k // 2 + 1)
            PASSES = ((0, 0), (0, 1), (1, 0))

            def mod(c):
                n = place["mod", c]
                if c >= 2:
                    pe.wait_ge(S["mod_row"], c - 1)
                for k in range(KC):
                    part_ready(n, k)
                    for s, m in PASSES:
                        ins = mm(ps[0:2, (4 if c < MOD_EARLY else 6) + c % 2, :], conds[:, s, k, :], weight(n, k, m),
                                 start=(k == 0 and s + m == 0), stop=(k == KC - 1 and s == 1))
                ins.then_inc(S["mod_mm"], 1)

            def mod_cols(c):
                pe.wait_ge(S["mod_row"], c + 1)
                for j in range(4):
                    o = (4 * c + j) * 2
                    ins = mm(ps[:, 6, o:o + 2], mod_mem(c)[2][:, j * P:(j + 1) * P], ident[0:2, 0:2], start=True, stop=True)
                ins.then_inc(S["col_mm"], 1)

            pe.wait_ge(S["consts"], 5)
            pe.wait_ge(S["conds_lo"], 1)
            mod(0)
            for c in range(1, MOD_EARLY):
                mod(c)
                mod_cols(c - 1)
            mod_cols(MOD_EARLY - 1)
            pe.wait_ge(S["xn_ready"], TB)
            for k in range(KC):
                if k >= 2:
                    pe.wait_ge(S["hT_lat"], k - 1)
                    pe.wait_ge(S["hT_ctx"], k - 1)
                for b in range(4):
                    nc.tensor.transpose(ps[:, 2 * (k % 2), b * P:(b + 1) * P], xn[:, b, k * P:(k + 1) * P], ident[:, :])
                nc.tensor.transpose(ps[:, 2 * (k % 2) + 1, 0:P], xn[:, CTX, k * P:(k + 1) * P], ident[:, :]).then_inc(S["h_tr"], 1)
            pe.wait_ge(S["hT_lat"], KC)
            pe.wait_ge(S["hT_ctx"], KC)

            def transpose_rows(g):
                pe.wait_ge(S["roped"], g + 1)
                if g >= 2:
                    pe.wait_ge(S["qkT"], g - 1)
                for h in range(H):
                    ins = nc.tensor.transpose(ps[:, 2 + g % 2, h * P:(h + 1) * P], qr(g)[:, h * P:(h + 1) * P], ident[:, :])
                ins.then_inc(S["qk_tr"], 1)
            for g in range(3 * TB):
                part, b = g // TB, g % TB
                n = place["in", part]
                if 2 <= g < 2 * TB + 2:
                    pe.wait_ge(S["roped"], g - 1)
                elif g >= 2:
                    pe.wait_ge(S["v_done"], g - 2 * TB - 1)
                for k in range(KC):
                    part_ready(n, k)
                    for s, m in PASSES:
                        ins = mm(ps[:, g % 2, :], hS[:, s, k, b * P:(b + 1) * P], weight(n, k, m),
                                 start=(k == 0 and s + m == 0), stop=(k == KC - 1 and s == 1))
                ins.then_inc(S["z_mm"], 1)
                if 1 <= g <= 2 * TB:
                    transpose_rows(g - 1)
            pe.wait_ge(S["ck_in"], 16)
            for h in range(H):
                ins = nc.tensor.transpose(ps[:, 6, h * P:(h + 1) * P], ck[:, h, :], ident[:, :])
            ins.then_inc(S["qk_tr"], 1)
            pe.wait_ge(S["v_done"], TB)
            pe.wait_ge(S["qkT"], 2 * TB + 1)
            pe.wait_ge(S["cv_in"], 16)

            def conv_part(g):
                cb, j = g // 3, g % 3
                n, part = place["conv", cb], (1, 2, 0)[j]
                if g >= 1:
                    if j == 1:
                        pe.wait_ge(S["conv_c"], 2 * cb + 2)
                    elif j == 2:
                        pe.wait_ge(S["conv_u"], 2 * cb + 2)
                    else:
                        pe.wait_ge(S["conv_y"], 2 * cb)
                for k in range(KC):
                    part_ready(n, k)
                    for s, m in PASSES:
                        w = conv_weight(n, k, s, part)
                        ends = dict(start=(k == 0 and s + m == 0), stop=(k == KC - 1 and s == 1))
                        mm(ps[:, 6, :], w, hS[:, m, k, 0:L_LAT], **ends)
                        ins = mm(ps[:, 7, 0:P], w, hS[:, m, k, L_LAT:TOK], **ends)
                ins.then_inc(S["conv_mm"], 1)

            def scores(u):
                h, b = UNITS[u]
                for c in range(2):
                    if u >= 1:
                        pe.wait_ge(S[f"exp{c}"], u)
                    q = qT[c * DQ:(c + 1) * DQ, h, b * P:(b + 1) * P]
                    if b < CTX:
                        mm(ps[:, 2 * c, :], q, kT[c * DQ:(c + 1) * DQ, h, 0:N], start=True, stop=True)
                        ins = mm(ps[:, 2 * c + 1, 0:P], q, kT[c * DQ:(c + 1) * DQ, h, N:KEYS], start=True, stop=True)
                    else:
                        ins = mm(ps[:, 2 * c, 0:P], q, kT[c * DQ:(c + 1) * DQ, h, KEYS:KEYS + P], start=True, stop=True)
                    ins.then_inc(S["s_mm"], 1)

            def lat_units(u):
                return sum(1 for h, b in UNITS[:u + 1] if b < CTX)

            def p_transposes(u):
                nb = 5 if UNITS[u][1] < CTX else 1
                pe.wait_ge(S["p_ready"], u + 1)
                if u >= 1:
                    pe.wait_ge(S["pt_act"], u)
                    pe.wait_ge(S["pt_dve"], lat_units(u - 1))
                    pe.wait_ge(S["o_evac"], u)
                for j in range(nb):
                    ins = nc.tensor.transpose(ps[:, 4 + j // 4, (j % 4) * P:(j % 4 + 1) * P], p_buf(u)[:, j * P:(j + 1) * P], ident[:, :])
                ins.then_inc(S["p_tr"], 1)

            def pv(u):
                h, b = UNITS[u]
                pe.wait_ge(S["pt_act"], u + 1)
                pe.wait_ge(S["pt_dve"], lat_units(u))
                nb = 5 if b < CTX else 1
                for j in range(nb):
                    kb = j if b < CTX else 5
                    ins = mm(ps[:, 5, P:2 * P], V[:, kb, h * P:(h + 1) * P], pt_buf(u)[:, j * P:(j + 1) * P],
                             start=(j == 0), stop=(j == nb - 1))
                ins.then_inc(S["pv_mm"], 1)

            def head_squares(h):
                pe.wait_ge(S["osq"], h + 1)
                mm(ps[:, 6, :], ones[:, :], osq_buf[:, 0:N], start=True, stop=True)
                mm(ps[:, 7, 0:P], ones[:, :], osq_buf[:, N:TOK], start=True, stop=True).then_inc(S["osq_mm"], 1)

            def banks_left(u):
                if u <= 12:
                    g = u - 1
                    pe.wait_ge(*((S["conv_c"], 2 * (g // 3) + 2), (S["conv_u"], 2 * (g // 3) + 2),
                                 (S["conv_y"], 2 * (g // 3) + 2))[g % 3])
                else:
                    pe.wait_ge(S["mod_row"], MOD_EARLY + u - 12)
            for u in range(len(UNITS)):
                scores(u)
                if u >= 1:
                    pv(u - 1)
                if u in ROOT_STEP:
                    banks_left(u)
                    head_squares(ROOT_STEP[u])
                    pe.wait_ge(S["osr"], ROOT_STEP[u] + 1)
                if u < 12:
                    conv_part(u)
                else:
                    if u == 12:
                        banks_left(u)
                    mod(u - 12 + MOD_EARLY)
                p_transposes(u)
            pv(len(UNITS) - 1)
            banks_left(len(UNITS))
            head_squares(H - 1)

            def router(b):
                pe.wait_ge(S["h2s"], b + 1)
                if b >= 1:
                    pe.wait_ge(S["h2T_ev"], b)
                for k in range(KC):
                    ins = nc.tensor.transpose(ps[:, 4 + k // 4, (k % 4) * P:(k % 4 + 1) * P], h2[:, b, k * P:(k + 1) * P], ident[:, :])
                ins.then_inc(S["h2_tr"], 1)
                pe.wait_ge(S["h2T_ev"], b + 1)
                for k in range(KC):
                    ins = mm(ps[:, 6, b * 20:(b + 1) * 20], work[:, k * P:(k + 1) * P], wr[:, k, :], start=(k == 0), stop=(k == KC - 1))
                ins.then_inc(S["lg_mm"], 1)
            pe.wait_ge(S["wr_in"], 32)
            pe.wait_ge(S["mod_row"], N_MOD)
            for b in range(TB):
                if b >= 2:
                    pe.wait_ge(S["x2s"], b - 1)
                for n, k in enumerate(CAT_ORDER):
                    if b == 0:
                        pe.wait_ge(S["cat_lo"], n + 1)
                    for j in range(2):
                        pe.wait_ge(S["lo"], 4 * place["o", j] + k // 2 + 1)
                        for s, m in PASSES:
                            ins = mm(ps[:, 2 * (b % 2) + j, :], hS[:, s, k, b * P:(b + 1) * P], weight(place["o", j], k, m),
                                     start=(n == 0 and s + m == 0), stop=(n == KC - 1 and s == 1))
                ins.then_inc(S["wo_mm"], 1)
                if b >= 1:
                    router(b - 1)
            router(TB - 1)
            pe.wait_ge(S["oh_ready"], 1)
            A = rw["A"].rearrange("p (b n) -> p b n", b=TB)
            for b in range(TB):
                for j in range(b):
                    mm(ps[:, 7, b * 16:(b + 1) * 16], ones[:, :], A[:, j, :], start=(j == 0), stop=False)
                mm(ps[:, 7, b * 16:(b + 1) * 16], tri[:, :], A[:, b, :], start=(b == 0), stop=True)
            for j in range(TB):
                ins = mm(ps[:, 7, 80:96], ones[:, :], A[:, j, :], start=(j == 0), stop=(j == TB - 1))
            ins.then_inc(S["cum_mm"], 1)
            def x_transposes(tile):
                p = tile[1] % 2
                i, c = tile
                pe.wait_ge(S[f"xs_in{p}"], 16 * (c // 2) + 16 if i is None else 16 * i + (16 * (c // 2) + 16))
                for k in range(KC):
                    ins = nc.tensor.transpose(ps[:, 2 + k // 4, (k % 4) * P:(k % 4 + 1) * P], xtile[p][:, k * P:(k + 1) * P], ident[:, :])
                ins.then_inc(S["xs_tr"], 1)

            def gate_up(tile):
                pe.wait_ge(S["xT_lo"], lin(tile, 2, 2))
                for j in range(2):
                    for k in range(KC):
                        if k % 2 == 0:
                            pe.wait_ge(S["lo"], moe_lo(tile, j, k // 2))
                        slot = moe_split_slot(tile, j, k // 2)
                        for s, m in PASSES:
                            ins = mm(ps[:, j, :], xS[:, s, k, :], spl[:, slot, m, (k % 2) * N:(k % 2 + 1) * N],
                                     start=(k == 0 and s + m == 0), stop=(k == KC - 1 and s == 1))
                        if k % 2:
                            ins.then_inc(S[("g_mm", "u_mm")[j]], 1)

            def a_transposes(tile):
                pe.wait_ge(S["act_a"], lin(tile, 1, 1))
                for k in range(4):
                    ins = nc.tensor.transpose(ps[:, 4, k * P:(k + 1) * P], act_rows[:, k * P:(k + 1) * P], ident[:, :])
                ins.then_inc(S["a_tr"], 1)

            def down(tile, turn, j):
                pe.wait_ge(S["aT_lo"], lin(tile, 1, 1))
                if tile[0] is not None or tile[1] > 0:
                    pe.wait_ge(S["o_act"], lin(tile, 1, 0))
                for k in range(4):
                    pe.wait_ge(S["lo"], moe_lo(turn, j, k))
                    for half in range(2):
                        for s, m in PASSES:
                            ins = mm(ps[:, 5 + half, :], aS[:, s, k, :], spl[:, moe_split_slot(turn, j, k), m, half * N:(half + 1) * N],
                                     start=(k == 0 and s + m == 0), stop=(k == 3 and s == 1))
                    ins.then_inc(S["dn_mm"], 1)

            def expert_tile(tile):
                gate_up(tile)
                x_transposes((tile[0], tile[1] + 1))
                down((tile[0], tile[1] - 1), tile, 2)
                a_transposes(tile)
            pe.wait_ge(S["steer_ready"], 1)
            x_transposes((None, 0))
            gate_up((None, 0))
            x_transposes((None, 1))
            a_transposes((None, 0))
            expert_tile((None, 1))
            later = pe.value_load(steer[0:1, 30:31], min_val=NEXP // 2 - 1, max_val=MAX_PAIRS - 1)
            with pe.Fori(0, later) as i:
                expert_tile((i, 2))
                expert_tile((i, 3))
            down((later, 1), (later, 2), 0)


_INS = ["x_prompt", "x_sample", "cache_k", "cache_v", "c", "c_ctx", "w_mod", "b_mod", "g_pre1", "g_post1", "g_pre2",
        "g_post2", "w_in", "conv_w", "lambda_q1", "lambda_k1", "lambda_q2", "lambda_k2", "subln_g", "w_o",
        "w_router_group", "w_router_expert", "w_exp_gate", "w_exp_up", "w_exp_down"]
_OUTS = [("out_ctx", (1, 128, 1024)), ("out_lat", (1, 512, 1024)),
         ("out_k", (1, 1, 4, 128, 128)), ("out_v", (1, 1, 4, 128, 128))]


def rope_tables():
    import numpy as np
    t = np.arange(L_LAT)
    inv = (np.float32(10000.0) ** (-np.arange(16, dtype=np.float32) / np.float32(16))).astype(np.float32)
    ar = (t // 64).astype(np.float32)[:, None] * inv
    ac = (t % 64).astype(np.float32)[:, None] * inv
    ang = np.concatenate([ar, ar, ac, ac], -1)
    sign = np.concatenate([-np.ones(16), np.ones(16)] * 2).astype(np.float32)
    return np.stack([np.cos(ang), np.sin(ang) * sign]).astype(np.float32)


def kernel(**inputs):
    import numpy as np
    import concourse.bacc as bacc
    from concourse.bass_utils import run_bass_kernel_spmd

    nc = bacc.Bacc("TRN2", target_bir_lowering=False, num_devices=1)
    arrays, aps = {}, {}
    for name in _INS:
        v = np.ascontiguousarray(inputs[name])
        arrays[f"in_{name}"] = v
        aps[name] = nc.dram_tensor(f"in_{name}", v.shape, mybir.dt.from_np(v.dtype), kind="ExternalInput").ap()
    arrays["rope"] = rope_tables()
    aps["rope"] = nc.dram_tensor("rope", arrays["rope"].shape, F32, kind="ExternalInput").ap()
    for name, shape in _OUTS:
        aps[name] = nc.dram_tensor(name, shape, F32, kind="ExternalOutput").ap()
    build(nc, aps)
    r = run_bass_kernel_spmd(nc, [arrays], core_ids=[0])
    return tuple(r.results[0][name] for name, _ in _OUTS)
```
